# Optimizing a Trainium2 kernel written in Bass

```python
import math
import jax, jax.numpy as jnp
from jax import lax
import numpy as np

D_MODEL = 1024
BATCH = 1
SEQ = 256
DEPTH = 2

GRID_W = 64
CTX_LEN = 256
N_MIXERS = 4
N_MOD = 9
D_FF = 2816
NORM_EPS = 1e-6
POOL_WINDOWS = (2, 4, 8, 16)
POOL_GROUP = D_MODEL // len(POOL_WINDOWS)
CONV_WIDTH = 31
SHORT_CONV_WIDTH = 3
RET_HEADS = 8
RET_DK_HEAD = D_MODEL // RET_HEADS
RET_DV_HEAD = 2 * RET_DK_HEAD
RET_DK = RET_HEADS * RET_DK_HEAD
RET_DV = RET_HEADS * RET_DV_HEAD
RET_CHUNK = 128
ROPE_BASE = 10000.0
ROPE_SEQ_PAIRS = RET_DK_HEAD // 8
ROPE_GRID_PAIRS = (RET_DK_HEAD // 2 - ROPE_SEQ_PAIRS) // 2
LN2 = math.log(2.0)
N_POOL_LAYERS = (DEPTH + N_MIXERS - 1) // N_MIXERS
N_CONV_LAYERS = (DEPTH + N_MIXERS - 2) // N_MIXERS
N_RET_LAYERS = (DEPTH + N_MIXERS - 3) // N_MIXERS
N_SC_LAYERS = DEPTH // N_MIXERS
CTX_LAST_LAYER = DEPTH - 1 - (DEPTH - 3) % N_MIXERS

kernel_name = 'hybrid_interleaved_diffusion_backbone'

def _rmsnorm(x, g):
    xf = x.astype(jnp.float32)
    y = xf * lax.rsqrt(jnp.mean(xf * xf, axis=-1, keepdims=True) + NORM_EPS) * g.astype(jnp.float32)
    return y.astype(x.dtype)

def _adaln_params(cvec, w, b):
    return (jax.nn.silu(cvec) @ w + b).reshape(cvec.shape[0], N_MOD, D_MODEL)

def _modulated_norm(s, g, m, k):
    return _rmsnorm(s, g) * (1.0 + m[:, 3 * k + 1, None]) + m[:, 3 * k, None]

def _gate(m, k):
    return m[:, 3 * k + 2, None]

def _swiglu(h, wg, wu, wd):
    return (jax.nn.silu(h @ wg) * (h @ wu)) @ wd

def _half_ffn(s, g, m, k, wg, wu, wd):
    h = _modulated_norm(s, g, m, k)
    return s + 0.5 * _gate(m, k) * _swiglu(h, wg, wu, wd)

def _depthwise_conv(u, w):
    pad = (w.shape[0] - 1) // 2
    return lax.conv_general_dilated(u, w[:, None, :].astype(u.dtype), window_strides=(1,),
                                    padding=[(pad, pad)], dimension_numbers=('NWC', 'WIO', 'NWC'),
                                    feature_group_count=u.shape[-1])

def _pool_mixer(h, w_grp, scale):
    B, L, _ = h.shape
    hf = h.astype(jnp.float32)
    cs = jnp.pad(jnp.cumsum(hf, axis=1), ((0, 0), (1, 0), (0, 0)))
    t = jnp.arange(L)
    groups = []
    for g, w in enumerate(POOL_WINDOWS):
        lo = jnp.clip(t - w // 2, 0, L)
        hi = jnp.clip(t + w // 2, 0, L)
        sl = slice(g * POOL_GROUP, (g + 1) * POOL_GROUP)
        csg = cs[..., sl]
        mean = (csg[:, hi] - csg[:, lo]) / (hi - lo).astype(jnp.float32)[None, :, None]
        groups.append(mean - hf[..., sl])
    p = jnp.stack(groups, axis=2).astype(h.dtype)
    y = jnp.einsum('blgc,gcd->blgd', p, w_grp).reshape(B, L, D_MODEL)
    return y * scale

def _conformer_conv(h, w_in, dw, ln_g, ln_b, w_out):
    a, b = jnp.split(h @ w_in, 2, axis=-1)
    u = _depthwise_conv(a * jax.nn.sigmoid(b), dw)
    uf = u.astype(jnp.float32)
    mu = jnp.mean(uf, axis=-1, keepdims=True)
    var = jnp.mean(jnp.square(uf - mu), axis=-1, keepdims=True)
    u = ((uf - mu) * lax.rsqrt(var + NORM_EPS) * ln_g.astype(jnp.float32) + ln_b.astype(jnp.float32)).astype(h.dtype)
    return jax.nn.silu(u) @ w_out

def _short_conv(h, w_in, conv_w, w_out):
    b, cg, u = jnp.split(h @ w_in, 3, axis=-1)
    return (b * _depthwise_conv(cg * u, conv_w)) @ w_out

def _rope_angles(p_seq, p_row, p_col):
    f_seq = ROPE_BASE ** (-jnp.arange(ROPE_SEQ_PAIRS, dtype=jnp.float32) / ROPE_SEQ_PAIRS)
    f_grid = ROPE_BASE ** (-jnp.arange(ROPE_GRID_PAIRS, dtype=jnp.float32) / ROPE_GRID_PAIRS)
    return jnp.concatenate([p_seq[:, None] * f_seq, p_row[:, None] * f_grid, p_col[:, None] * f_grid], axis=-1)

def _rope(x, ang):
    half = x.shape[-1] // 2
    cos = jnp.cos(ang)[None, :, None, :]
    sin = jnp.sin(ang)[None, :, None, :]
    x1, x2 = x[..., :half], x[..., half:]
    return jnp.concatenate([x1 * cos - x2 * sin, x1 * sin + x2 * cos], axis=-1)

def _heads(a, d):
    return a.reshape(a.shape[0], a.shape[1], RET_HEADS, d).astype(jnp.float32)

def _ret_project(h, w_in, ang, with_query):
    if not with_query:
        kv = h @ w_in[:, RET_DK:2 * RET_DK + RET_DV]
        return _rope(_heads(kv[..., :RET_DK], RET_DK_HEAD), ang), _heads(kv[..., RET_DK:], RET_DV_HEAD)
    proj = h @ w_in
    q = _rope(_heads(proj[..., :RET_DK], RET_DK_HEAD), ang) * (RET_DK_HEAD ** -0.5)
    k = _rope(_heads(proj[..., RET_DK:2 * RET_DK], RET_DK_HEAD), ang)
    v = _heads(proj[..., 2 * RET_DK:2 * RET_DK + RET_DV], RET_DV_HEAD)
    g = proj[..., 2 * RET_DK + RET_DV:]
    return k, v, q, g

def _retention_scan(q, k, v, log_gamma, s0):
    B, L, H, _ = q.shape
    dv = v.shape[-1]
    n = L // RET_CHUNK

    def chunks(a):
        return a.reshape(B, n, RET_CHUNK, H, a.shape[-1]).transpose(1, 0, 3, 2, 4)

    i = jnp.arange(RET_CHUNK, dtype=jnp.float32)
    diff = i[:, None] - i[None, :]
    lower = diff >= 0
    dmat = jnp.where(lower, jnp.exp(jnp.where(lower, diff, 0.0)[None] * log_gamma[:, None, None]), 0.0)
    q_dec = jnp.exp((i + 1.0)[None, :] * log_gamma[:, None])[:, :, None]
    k_dec = jnp.exp((RET_CHUNK - 1.0 - i)[None, :] * log_gamma[:, None])[:, :, None]
    chunk_dec = jnp.exp(RET_CHUNK * log_gamma)[:, None, None]

    def step(s, qkv):
        qc, kc, vc = qkv
        scores = jnp.einsum('bhqd,bhkd->bhqk', qc, kc) * dmat
        y = jnp.einsum('bhqk,bhkv->bhqv', scores, vc) + jnp.einsum('bhqd,bhdv->bhqv', qc * q_dec, s)
        s = s * chunk_dec + jnp.einsum('bhkd,bhkv->bhdv', kc * k_dec, vc)
        return s, y

    _, y = lax.scan(step, s0, (chunks(q), chunks(k), chunks(v)))
    return y.transpose(1, 0, 3, 2, 4).reshape(B, L, H, dv)

def _bidirectional(q, k, v, lg, s_fwd, s_bwd):
    y_f = _retention_scan(q, k, v, lg[0], s_fwd)
    y_b = _retention_scan(q[:, ::-1], k[:, ::-1], v[:, ::-1], lg[1], s_bwd)[:, ::-1]
    return y_f + y_b

def _ret_output(y, g, gn_g, w_out):
    B, L = y.shape[:2]
    mu = jnp.mean(y, axis=-1, keepdims=True)
    var = jnp.mean(jnp.square(y - mu), axis=-1, keepdims=True)
    yn = ((y - mu) * lax.rsqrt(var + NORM_EPS)).reshape(B, L, RET_DV) * gn_g.astype(jnp.float32)
    return (jax.nn.silu(g) * yn.astype(g.dtype)) @ w_out

def _retention_mixer(hx, hc, w_in, log_eps, gn_g, w_out, with_ctx_out):
    lg = jnp.log1p(-jnp.exp(log_eps.astype(jnp.float32)))
    Lx, Lc = hx.shape[1], hc.shape[1]
    rows = Lx // GRID_W
    ang_x = _rope_angles(jnp.full((Lx,), float(CTX_LEN), jnp.float32),
                         jnp.repeat(jnp.arange(rows, dtype=jnp.float32), GRID_W),
                         jnp.tile(jnp.arange(GRID_W, dtype=jnp.float32), rows))
    pc = jnp.arange(Lc, dtype=jnp.float32)
    ang_c = _rope_angles(pc, jnp.zeros_like(pc), jnp.zeros_like(pc))
    kx, vx, qx, gx = _ret_project(hx, w_in, ang_x, True)
    if with_ctx_out:
        kc, vc, qc, gc = _ret_project(hc, w_in, ang_c, True)
    else:
        kc, vc = _ret_project(hc, w_in, ang_c, False)
    s_fwd = jnp.einsum('bmhd,hm,bmhv->bhdv', kc, jnp.exp((Lc - 1.0 - pc)[None, :] * lg[0][:, None]), vc)
    s_bwd = jnp.einsum('bmhd,hm,bmhv->bhdv', kc, jnp.exp(pc[None, :] * lg[1][:, None]), vc)
    y_lat = _ret_output(_bidirectional(qx, kx, vx, lg, s_fwd, s_bwd), gx, gn_g, w_out)
    if with_ctx_out:
        zero = jnp.zeros_like(s_fwd)
        y_ctx = _ret_output(_bidirectional(qc, kc, vc, lg, zero, zero), gc, gn_g, w_out)
        return y_lat, y_ctx
    return y_lat, None

def setup_inputs(seed: int = 0) -> dict:
    key = jax.random.key(seed)
    ks = jax.random.split(key, 25)
    D = D_MODEL

    def nrm(k, shape, scale):
        return jax.random.normal(k, shape, jnp.float32) * scale

    base_log_eps = -(5.0 + jnp.arange(RET_HEADS, dtype=jnp.float32)) * LN2
    return {
        'x': nrm(ks[0], (BATCH, SEQ, D), 1.0),
        'c': nrm(ks[1], (BATCH, D), 1.0),
        'ctx': nrm(ks[2], (BATCH, CTX_LEN, D), 1.0),
        'c_ctx': nrm(ks[3], (D,), 1.0),
        'mod_w': nrm(ks[4], (DEPTH, D, N_MOD * D), 0.5 * D ** -0.5),
        'mod_b': nrm(ks[5], (DEPTH, N_MOD * D), 0.02),
        'norm_g': 1.0 + nrm(ks[6], (DEPTH, 3, D), 0.05),
        'final_g': 1.0 + nrm(ks[7], (D,), 0.05),
        'ffn_w_gate': nrm(ks[8], (DEPTH, 2, D, D_FF), D ** -0.5),
        'ffn_w_up': nrm(ks[9], (DEPTH, 2, D, D_FF), D ** -0.5),
        'ffn_w_down': nrm(ks[10], (DEPTH, 2, D_FF, D), D_FF ** -0.5),
        'pool_w': nrm(ks[11], (N_POOL_LAYERS, len(POOL_WINDOWS), POOL_GROUP, POOL_GROUP), POOL_GROUP ** -0.5),
        'pool_scale': 1.0 + nrm(ks[12], (N_POOL_LAYERS, D), 0.1),
        'conv_w_in': nrm(ks[13], (N_CONV_LAYERS, D, 2 * D), D ** -0.5),
        'conv_dw': nrm(ks[14], (N_CONV_LAYERS, CONV_WIDTH, D), CONV_WIDTH ** -0.5),
        'conv_ln_g': 1.0 + nrm(ks[15], (N_CONV_LAYERS, D), 0.05),
        'conv_ln_b': nrm(ks[16], (N_CONV_LAYERS, D), 0.02),
        'conv_w_out': nrm(ks[17], (N_CONV_LAYERS, D, D), D ** -0.5),
        'ret_w_in': nrm(ks[18], (N_RET_LAYERS, D, 2 * RET_DK + 2 * RET_DV), D ** -0.5),
        'ret_log_eps': base_log_eps[None, None, :] + nrm(ks[19], (N_RET_LAYERS, 2, RET_HEADS), 0.1),
        'ret_gn_g': 1.0 + nrm(ks[20], (N_RET_LAYERS, RET_DV), 0.05),
        'ret_w_out': nrm(ks[21], (N_RET_LAYERS, RET_DV, D), RET_DV ** -0.5),
        'sc_w_in': nrm(ks[22], (N_SC_LAYERS, D, 3 * D), D ** -0.5),
        'sc_conv': nrm(ks[23], (N_SC_LAYERS, SHORT_CONV_WIDTH, D), SHORT_CONV_WIDTH ** -0.5),
        'sc_w_out': nrm(ks[24], (N_SC_LAYERS, D, D), D ** -0.5),
    }

def reference(x, c, ctx, c_ctx, mod_w, mod_b, norm_g, final_g, ffn_w_gate, ffn_w_up, ffn_w_down,
              pool_w, pool_scale, conv_w_in, conv_dw, conv_ln_g, conv_ln_b, conv_w_out,
              ret_w_in, ret_log_eps, ret_gn_g, ret_w_out, sc_w_in, sc_conv, sc_w_out):
    for i in range(DEPTH):
        kind, j = i % N_MIXERS, i // N_MIXERS
        ctx_live = i <= CTX_LAST_LAYER
        ctx_full = i < CTX_LAST_LAYER
        m_x = _adaln_params(c, mod_w[i], mod_b[i])
        m_c = _adaln_params(c_ctx[None], mod_w[i], mod_b[i]) if ctx_live else None

        ffn1 = (ffn_w_gate[i, 0], ffn_w_up[i, 0], ffn_w_down[i, 0])
        x = _half_ffn(x, norm_g[i, 0], m_x, 0, *ffn1)
        if ctx_live:
            ctx = _half_ffn(ctx, norm_g[i, 0], m_c, 0, *ffn1)

        hx = _modulated_norm(x, norm_g[i, 1], m_x, 1)
        hc = _modulated_norm(ctx, norm_g[i, 1], m_c, 1) if ctx_live else None
        if kind == 2:
            yx, yc = _retention_mixer(hx, hc, ret_w_in[j], ret_log_eps[j], ret_gn_g[j], ret_w_out[j], ctx_full)
        else:
            if kind == 0:
                mix = lambda h: _pool_mixer(h, pool_w[j], pool_scale[j])
            elif kind == 1:
                mix = lambda h: _conformer_conv(h, conv_w_in[j], conv_dw[j], conv_ln_g[j], conv_ln_b[j], conv_w_out[j])
            else:
                mix = lambda h: _short_conv(h, sc_w_in[j], sc_conv[j], sc_w_out[j])
            yx = mix(hx)
            yc = mix(hc) if ctx_full else None
        x = x + _gate(m_x, 1) * yx
        if ctx_full:
            ctx = ctx + _gate(m_c, 1) * yc

        ffn2 = (ffn_w_gate[i, 1], ffn_w_up[i, 1], ffn_w_down[i, 1])
        x = _half_ffn(x, norm_g[i, 2], m_x, 2, *ffn2)
        if ctx_full:
            ctx = _half_ffn(ctx, norm_g[i, 2], m_c, 2, *ffn2)
    return _rmsnorm(x, final_g)


_drawn_inputs = setup_inputs


def setup_inputs(seed=0):
    import zlib

    import numpy as np

    out = dict(_drawn_inputs(seed))
    spreads = {}
    factors = {'conv_ln_g': 5.436, 'conv_ln_b': 8.0}
    for name, (base, spread) in spreads.items():
        noise = np.random.default_rng([zlib.crc32(name.encode()), seed]).standard_normal(out[name].shape)
        drawn = base * np.exp(spread * noise) if base else spread * noise
        out[name] = __import__('jax').numpy.asarray(drawn.astype(out[name].dtype))
    for name, factor in factors.items():
        out[name] = (out[name] * factor).astype(out[name].dtype)
    return out
```

```python
from contextlib import ExitStack

import concourse.bass as bass
from concourse import mybir

ALU = mybir.AluOpType
ACT = mybir.ActivationFunctionType
F32 = mybir.dt.float32
F32R = mybir.dt.float32r

P = 128
EPS = 1e-6
POOL_WINDOWS = (2, 4, 8, 16)
PAD = 15
MOD_COLS = 512
BLK = 256
SUB = BLK // P
DIAG_SLOTS = 8
CONV_TILES_ON_PE = (5, 6, 7)


def backbone_kernel(nc, x, c, mod_w, mod_b, norm_g, final_g, ffn_w_gate, ffn_w_up, ffn_w_down,
                    pool_w, pool_scale, conv_w_in, conv_dw, conv_ln_g, conv_ln_b, conv_w_out, out):
    _, L, D = x.shape
    DEPTH, _, _, FF = ffn_w_gate.shape
    TAPS = conv_dw.shape[1]
    KT = D // P
    NB = FF // BLK
    NC = D // BLK
    PAIRS = KT // 2
    N_MOD = mod_w.shape[2] // D
    MOD_UNITS = N_MOD * D // MOD_COLS
    MOD_SUB = MOD_COLS // P
    WIDTH = L + 2 * PAD
    LOOPS = (NB - 3) // 2
    assert DEPTH == 2 and L == 256 and KT == 8 and NB == 11 and NC == 4 and TAPS == 2 * PAD + 1
    assert MOD_UNITS == 18

    G0 = [0, NB + 1, 2 * NB + 1, 3 * NB + 1 + NC]
    U0 = [0, NB, 2 * NB, 3 * NB + NC]
    D0 = [0, NB, 2 * NB, 3 * NB + NC]
    GC, UC, DC = 3 * NB + 1, 3 * NB, 3 * NB
    MOD_PRE = [4, 16, 26, None]
    MOD_AT = [5, 17, 27, None]
    MOD_LAST = [NB - 1, NB - 3, NB - 3, -1]

    NORM_G, FINAL_G = 0, DEPTH * 3 * KT
    POOL_SC, LN_G, LN_B, C_COL = (FINAL_G + (j + 1) * KT for j in range(4))
    MOD_B = C_COL + KT
    DW = MOD_B + DEPTH * N_MOD * KT
    N_COLS = DW + TAPS * KT

    with ExitStack() as ctx:
        def sb(name, shape, dt=F32):
            return ctx.enter_context(nc.sbuf_tensor(name, shape, dt))

        def psum(name, shape):
            return ctx.enter_context(nc.psum_tensor(name, shape, F32))

        def sem(name):
            return ctx.enter_context(nc.semaphore(name))

        g_raw, u_raw = sb("g_raw", [P, 2, KT, BLK]), sb("u_raw", [P, 2, KT, BLK])
        d_raw = sb("d_raw", [P, SUB, D])
        g_hi, g_lo = sb("g_hi", [P, 2, KT, BLK], F32R), sb("g_lo", [P, 2, KT, BLK], F32R)
        u_hi, u_lo = sb("u_hi", [P, 2, KT, BLK], F32R), sb("u_lo", [P, 2, KT, BLK], F32R)
        d_hi, d_lo = sb("d_hi", [P, 2, SUB, D], F32R), sb("d_lo", [P, 2, SUB, D], F32R)
        m_raw = sb("m_raw", [P, 2, KT // 2, MOD_COLS])
        xs = sb("xs", [P, KT, L])
        wide = sb("wide", [P, KT, WIDTH])
        h_hi, h_lo = sb("h_hi", [P, KT, L], F32R), sb("h_lo", [P, KT, L], F32R)
        a_hi, a_lo = sb("a_hi", [P, 2, SUB, L], F32R), sb("a_lo", [P, 2, SUB, L], F32R)
        scr = sb("scr", [P, 2048])
        cols = sb("cols", [P, N_COLS])
        mcol = sb("mcol", [P, DEPTH * N_MOD * KT])
        acc = sb("acc", [P, MOD_COLS])
        csilu = sb("csilu", [P, KT])
        coef = sb("coef", [P, KT])
        gcoef = sb("gcoef", [P, KT])
        edge = sb("edge", [P, len(POOL_WINDOWS), 2, max(POOL_WINDOWS) // 2])
        eps = sb("eps", [P, 1])
        one = sb("one", [P, 1])
        mean_w = sb("mean_w", [P, P])
        ident = sb("ident", [P, P])

        x_rows = d_raw[:]
        out_rows = d_raw[:]
        conv = m_raw[:].rearrange("p a k n -> p (a k n)")[:, 0:KT * L].rearrange("p (k t) -> p k t", k=KT)
        vec_rows = scr[:, 0:5 * P].rearrange("p (r n) -> p r n", r=5)
        gated = scr[:, 0:512]
        prod = scr[:, 512:1024]
        sq = [scr[:, 512 * j:512 * (j + 1)] for j in range(2)]
        root, rstd = scr[:, 1024:1280], scr[:, 1280:1536]
        scaled = [scr[:, 1536 + 256 * j:1792 + 256 * j] for j in range(2)]
        run_sum = [scr[:, 544 * j:544 * (j + 1)].rearrange("p (k t) -> p k t", k=2) for j in range(2)]
        diag = scr[:, 1024:1024 + DIAG_SLOTS * P].rearrange("p (s n) -> p s n", s=DIAG_SLOTS)

        ps_g, ps_u, ps_mod, ps_stat = (psum(n, [P, 512]) for n in ("ps_g", "ps_u", "ps_mod", "ps_stat"))
        ps_d = psum("ps_d", [P, PAIRS, 512])
        CONV_BANK = dict(zip(CONV_TILES_ON_PE, (3, 2, 0)))

        x_in, vec_in, stored = sem("x_in"), sem("vec_in"), sem("stored")
        g_in, u_in = [sem("g_in0"), sem("g_in1")], [sem("u_in0"), sem("u_in1")]
        m_in, d_in = [sem("m_in0"), sem("m_in1")], sem("d_in")
        s_g_hi, s_g_lo, s_u_hi, s_u_lo = sem("g_hi_ready"), sem("g_lo_ready"), sem("u_hi_ready"), sem("u_lo_ready")
        s_d_hi, s_d_lo = sem("d_hi_ready"), sem("d_lo_ready")
        gu_done, d_done = sem("gu_done"), sem("d_done")
        acc_step, reduced, mcol_ready = sem("acc_step"), sem("reduced"), sem("mcol_ready")
        gated_ready, prod_ready, a_hi_ready, a_lo_ready = (
            sem("gated_ready"), sem("prod_ready"), sem("a_hi_ready"), sem("a_lo_ready"))
        bank_ready, x_ready, sq_ready, stat_step = sem("bank_ready"), sem("x_ready"), sem("sq_ready"), sem("stat_step")
        root_ready, rstd_ready, coef_ready = sem("root_ready"), sem("rstd_ready"), sem("coef_ready")
        scaled_ready, operand_ready, h_hi_ready, h_lo_ready = (
            sem("scaled_ready"), sem("operand_ready"), sem("h_hi_ready"), sem("h_lo_ready"))
        consts_ready, consts_step, xt_ready, cols_psum, cols_ready, csilu_ready = (
            sem("consts_ready"), sem("consts_step"), sem("xt_ready"), sem("cols_psum"),
            sem("cols_ready"), sem("csilu_ready"))
        edge_step, pool_step = sem("edge_step"), sem("pool_step")
        glu_gate_ready, glu_ready, tap_step, diag_ready, diag_used, conv_ready = (
            sem("glu_gate_ready"), sem("glu_ready"), sem("tap_step"), sem("diag_ready"), sem("diag_used"),
            sem("conv_ready"))
        mu_ready, centred = sem("mu_ready"), sem("centred")
        out_psum, out_ready = sem("out_psum"), [sem("out_ready_dve"), sem("out_ready_act")]

        gate_v = ffn_w_gate.rearrange("l f (k p) n -> l f p k n", p=P)
        up_v = ffn_w_up.rearrange("l f (k p) n -> l f p k n", p=P)
        down_v = ffn_w_down.rearrange("l f (j p) n -> l f p j n", p=P)
        mod_v = mod_w.rearrange("l (k p) n -> l p k n", p=P)
        conv_in_v = conv_w_in.rearrange("l (k p) n -> l p k n", p=P)
        conv_out_v = conv_w_out.rearrange("l (j p) n -> l p j n", p=P)
        pool_v = pool_w.rearrange("l g (j p) n -> l p (g j) n", p=P)
        x_v = x.rearrange("b (a p) d -> (b p) a d", p=P)
        out_v = out.rearrange("b (a p) d -> (b p) a d", p=P)

        NORM_OF_STAGE = [0, 1, 2, 3, 4, 6, 7]
        LN_NORM = 5
        FFN_STAGE = [0, 2, 3, 5]
        FFN_LAYER = [0, 0, 1, 1]

        CONSTS = 4 + 2 * len(POOL_WINDOWS) + 1
        VEC_LOADS = 10

        def mod_at(layer, k):
            return (layer * N_MOD + k) * KT

        def f32(ap):
            return ap.bitcast(F32)

        block = ctx.enter_context(nc.Block())

        @block.sync
        def _(sp):
            def load_g(n, i, src):
                if n >= 2:
                    sp.wait_ge(s_g_lo, n - 1 + 2 * i)
                else:
                    sp.wait_ge(acc_step, 4 * (3 + n))
                sp.dma_start(g_raw[:, n % 2], src).then_inc(g_in[n % 2], 16)

            def load_u(n, i, src):
                if n >= 2:
                    sp.wait_ge(s_u_lo, n - 1 + 2 * i)
                else:
                    sp.wait_ge(acc_step, 4 * (5 + n))
                sp.dma_start(u_raw[:, n % 2], src).then_inc(u_in[n % 2], 16)

            def load_d(n, i, src):
                if n >= 1:
                    sp.wait_ge(s_d_lo, n + i * 2)
                else:
                    sp.wait_ge(xt_ready, PAIRS)
                sp.dma_start(d_raw[:], src).then_inc(d_in, 16)

            def load_mod(v, i):
                layer = v // MOD_UNITS
                for h in range(2):
                    src = mod_v[layer, :, 4 * h:4 * h + 4, bass.ds((v - layer * MOD_UNITS) * MOD_COLS + i * (2 * MOD_COLS), MOD_COLS)]
                    if v == 1:
                        sp.dma_start(g_raw[:, h].rearrange("p k n -> p (k n)").rearrange("p (k n) -> p k n", n=MOD_COLS), src).then_inc(g_in[h], 16)
                    elif v == 2:
                        sp.dma_start(u_raw[:, h].rearrange("p k n -> p (k n)").rearrange("p (k n) -> p k n", n=MOD_COLS), src).then_inc(u_in[h], 16)
                    else:
                        if v == 3:
                            sp.wait_ge(acc_step, 4 * (h + 1))
                        elif v >= 4:
                            sp.wait_ge(acc_step, 8 * v + 4 * h - 4 + 16 * i)
                        sp.dma_start(m_raw[:, h], src).then_inc(m_in[h], 16)

            def ffn_g(f, b, i=0):
                load_g(G0[f] + b, i, gate_v[FFN_LAYER[f], f % 2, :, :, bass.ds(b * BLK + i * (2 * BLK), BLK)])

            def ffn_u(f, b, i=0):
                load_u(U0[f] + b, i, up_v[FFN_LAYER[f], f % 2, :, :, bass.ds(b * BLK + i * (2 * BLK), BLK)])

            def ffn_d(f, b, i=0):
                load_d(D0[f] + b, i, down_v[FFN_LAYER[f], f % 2, :, bass.ds(b * SUB + i * (2 * SUB), SUB), :])

            def conv_g(b):
                load_g(GC + b, 0, conv_in_v[0, :, :, b * BLK:(b + 1) * BLK])

            def conv_u(b):
                load_u(UC + b, 0, conv_in_v[0, :, :, D + b * BLK:D + (b + 1) * BLK])

            def conv_d(b):
                load_d(DC + b, 0, conv_out_v[0, :, b * SUB:(b + 1) * SUB, :])

            def steady(f, b, i=0):
                ffn_g(f, b + 2, i)
                ffn_u(f, b + 2, i)
                ffn_d(f, b + 1, i)
                if b <= MOD_LAST[f]:
                    load_mod(MOD_AT[f] + b, i)

            def middle(f):
                steady(f, 0)
                with sp.Fori(0, LOOPS) as i:
                    steady(f, 1, i)
                    steady(f, 2, i)

            sp.dma_start(x_rows, x_v).then_inc(x_in, 16)
            for v in range(4):
                load_mod(v, 0)
            ffn_g(0, 0)
            ffn_g(0, 1)
            ffn_u(0, 0)
            ffn_u(0, 1)
            ffn_d(0, 0)
            load_mod(MOD_PRE[0], 0)
            middle(0)
            load_g(NB, 0, pool_v[0])
            ffn_u(1, 0)
            ffn_d(0, NB - 1)
            load_mod(MOD_AT[0] + NB - 2, 0)
            load_mod(MOD_AT[0] + NB - 1, 0)
            ffn_g(1, 0)
            ffn_u(1, 1)
            load_mod(MOD_PRE[1], 0)
            ffn_d(1, 0)
            ffn_g(1, 1)
            middle(1)
            ffn_g(2, 0)
            ffn_u(2, 0)
            ffn_d(1, NB - 1)
            ffn_g(2, 1)
            ffn_u(2, 1)
            ffn_d(2, 0)
            load_mod(MOD_PRE[2], 0)
            middle(2)
            conv_g(0)
            conv_u(0)
            ffn_d(2, NB - 1)
            conv_g(1)
            conv_u(1)
            conv_d(0)
            for b in range(2):
                conv_g(b + 2)
                conv_u(b + 2)
            conv_d(1)
            ffn_g(3, 0)
            ffn_u(3, 0)
            conv_d(2)
            ffn_g(3, 1)
            conv_d(3)
            ffn_u(3, 1)
            ffn_d(3, 0)
            middle(3)
            ffn_d(3, NB - 1)

            for n in range(PAIRS):
                sp.wait_ge(out_ready[n % 2], n // 2 + 1)
                cs = slice(n // 2 * (D // 2), (n // 2 + 1) * (D // 2))
                sp.dma_start(out_v[:, n % 2, cs], out_rows[:, n % 2, cs]).then_inc(stored, 16)
            sp.wait_ge(stored, 16 * PAIRS)

        @block.gpsimd
        def _(pool):
            nc.gpsimd.memset(ident[:], 0.0).then_inc(consts_step, 1)
            pool.wait_ge(consts_step, 1)
            nc.gpsimd.affine_select(out=ident[:], in_=ident[:], compare_op=ALU.not_equal, fill=1.0, base=0,
                                    pattern=[[-1, P]], channel_multiplier=1).then_inc(consts_ready, 1)
            nc.gpsimd.memset(mean_w[:], 1.0 / D).then_inc(consts_ready, 1)
            nc.gpsimd.memset(one[:], 1.0).then_inc(consts_ready, 1)
            nc.gpsimd.memset(eps[:], EPS).then_inc(consts_ready, 1)
            nc.gpsimd.memset(edge[:], 1.0).then_inc(consts_step, 1)
            pool.wait_ge(consts_step, 2)
            for g, w in enumerate(POOL_WINDOWS):
                nc.gpsimd.iota(edge[:, g, 0, 0:w // 2], pattern=[[1, w // 2]], base=w // 2, channel_multiplier=0,
                               allow_small_or_imprecise_dtypes=True).then_inc(consts_ready, 1)
                nc.gpsimd.iota(edge[:, g, 1, 0:w // 2], pattern=[[-1, w // 2]], base=w, channel_multiplier=0,
                               allow_small_or_imprecise_dtypes=True).then_inc(consts_ready, 1)
            nc.gpsimd.memset(wide[:], 0.0).then_inc(consts_ready, 1)

        @block.scalar
        def _(act):
            def hi_g(n, i=0):
                act.wait_ge(g_in[n % 2], 16 * (n // 2 + 2) + 16 * i)
                if n >= 2:
                    act.wait_ge(gu_done, n - 1 + 2 * i)
                nc.scalar.activation(g_hi[:, n % 2], g_raw[:, n % 2], ACT.Copy).then_inc(s_g_hi, 1)

            def hi_u(n, i=0):
                act.wait_ge(u_in[n % 2], 16 * (n // 2 + 2) + 16 * i)
                if n >= 2:
                    act.wait_ge(gu_done, (n - 1 if n - 2 < NB else n) + 2 * i)
                nc.scalar.activation(u_hi[:, n % 2], u_raw[:, n % 2], ACT.Copy).then_inc(s_u_hi, 1)

            def hi_d(n, i=0):
                act.wait_ge(d_in, 16 * (n + 1) + 32 * i)
                if n >= 2:
                    act.wait_ge(d_done, n - 1 + 2 * i)
                nc.scalar.activation(d_hi[:, n % 2], d_raw[:], ACT.Copy).then_inc(s_d_hi, 1)

            def block_out(f, b, i=0):
                e = NB * f + b
                act.wait_ge(gu_done, G0[f] + b + 1 + 2 * i)
                if e >= 1:
                    act.wait_ge(prod_ready, e + 2 * i)
                nc.scalar.activation(gated, ps_g[:], ACT.Silu).then_inc(gated_ready, 1)
                act.wait_ge(prod_ready, e + 1 + 2 * i)
                if b >= 2:
                    act.wait_ge(d_done, D0[f] + b - 1 + 2 * i)
                nc.scalar.activation(a_hi[:, b % 2].rearrange("p j t -> p (j t)"), prod, ACT.Copy).then_inc(a_hi_ready, 1)

            def steady(f, b, i=0):
                block_out(f, b, i)
                hi_g(G0[f] + b + 2, i)
                hi_u(U0[f] + b + 2, i)
                hi_d(D0[f] + b + 1, i)

            def middle(f):
                steady(f, 0)
                with act.Fori(0, LOOPS) as i:
                    steady(f, 1, i)
                    steady(f, 2, i)

            def norm_root(r, source, source_ready):
                nc.scalar.preload_act_table(ACT.Sqrt)
                for q in range(PAIRS):
                    act.wait_ge(*source_ready(q))
                    if q >= 2:
                        act.wait_ge(stat_step, PAIRS * r + q - 1)
                    nc.scalar.activation(sq[q % 2], source[:, 2 * q:2 * q + 2].rearrange("p k t -> p (k t)"),
                                         ACT.Square).then_inc(sq_ready, 1)
                act.wait_ge(stat_step, PAIRS * (r + 1))
                nc.scalar.activation(root, ps_stat[:, 0:L], ACT.Sqrt, bias=eps[:]).then_inc(root_ready, 1)
                nc.scalar.preload_act_table(ACT.Silu)

            def norm_hi(r):
                for k in range(KT):
                    act.wait_ge(operand_ready, KT * r + k + 1)
                    nc.scalar.activation(h_hi[:, k], wide[:, k, PAD:PAD + L], ACT.Copy).then_inc(h_hi_ready, 1)

            def stage(s, hi=True):
                r = NORM_OF_STAGE[s]
                norm_root(r, xs, lambda q: (x_ready, PAIRS * s + q + 1))
                if hi:
                    norm_hi(r)

            flat = lambda ap, s: ap.rearrange(s, n=P)
            A = vec_rows[:, 0]
            loads = [
                (A[NORM_G:FINAL_G], flat(norm_g, "l r (k n) -> (l r k) n")),
                (A[FINAL_G:POOL_SC], flat(final_g, "(k n) -> k n")),
                (A[POOL_SC:LN_G], flat(pool_scale, "l (k n) -> (l k) n")),
                (A[LN_G:LN_B], flat(conv_ln_g, "l (k n) -> (l k) n")),
                (A[LN_B:C_COL], flat(conv_ln_b, "l (k n) -> (l k) n")),
                (A[C_COL:MOD_B], flat(c, "b (k n) -> (b k) n")),
            ]
            half_dw = TAPS * KT // 2
            dw_rows = flat(conv_dw, "l w (k n) -> (l w k) n")
            for j in range(2):
                loads.append((vec_rows[0:N_MOD * KT, 1 + j], flat(mod_b[j], "(k n) -> k n")))
                loads.append((vec_rows[0:half_dw, 3 + j], dw_rows[j * half_dw:(j + 1) * half_dw]))
            for dst, src in loads:
                act.dma_start(dst, src).then_inc(vec_in, 16)
            assert len(loads) == VEC_LOADS
            nc.scalar.preload_act_table(ACT.Silu)
            act.wait_ge(cols_ready, 1)
            nc.scalar.activation(csilu[:], cols[:, C_COL:C_COL + KT], ACT.Silu).then_inc(csilu_ready, 1)
            act.wait_ge(consts_ready, CONSTS)
            norm_root(0, xs, lambda q: (x_ready, q + 1))
            hi_g(0)
            hi_g(1)
            hi_u(0)
            norm_hi(0)
            hi_u(1)
            hi_d(0)

            middle(0)
            block_out(0, NB - 2)
            hi_g(NB)
            hi_u(NB)
            hi_d(NB - 1)
            block_out(0, NB - 1)
            hi_g(NB + 1)
            stage(1)
            hi_u(NB + 1)
            stage(2)
            hi_d(NB)
            hi_g(NB + 2)

            middle(1)
            for b in (NB - 2, NB - 1):
                steady(1, b)
            stage(3)

            middle(2)
            for b in (NB - 2, NB - 1):
                steady(2, b)
            stage(4)

            nc.scalar.preload_act_table(ACT.Sigmoid)
            act.wait_ge(h_lo_ready, KT * 5)
            for b in range(NC):
                act.wait_ge(gu_done, GC + b + 1)
                if b >= 1:
                    act.wait_ge(glu_ready, 2 * b)
                src = ps_u[:] if b % 2 == 0 else ps_d[:, 1]
                nc.scalar.activation(gated, src, ACT.Sigmoid).then_inc(glu_gate_ready, 1)
                if b < NC - 2:
                    hi_g(GC + b + 2)
                    hi_u(UC + b + 2)
                if b == NC - 2:
                    hi_d(DC + 1)
            nc.scalar.preload_act_table(ACT.Silu)
            n = 0
            for t in CONV_TILES_ON_PE:
                for w in range(TAPS):
                    if n >= DIAG_SLOTS:
                        act.wait_ge(diag_used, n - DIAG_SLOTS + 1)
                    col = DW + w * KT + t
                    nc.scalar.activation(diag[:, n % DIAG_SLOTS], ident[:], ACT.Copy,
                                         scale=cols[:, col:col + 1]).then_inc(diag_ready, 1)
                    n += 1
            hi_g(G0[3])
            hi_u(U0[3])
            norm_root(LN_NORM, conv, lambda q: (centred, q + 1))
            for k in range(KT):
                act.wait_ge(scaled_ready, KT * LN_NORM + k + 1)
                nc.scalar.activation(wide[:, k, PAD:PAD + L], scaled[k % 2], ACT.Silu, scale=cols[:, LN_G + k:LN_G + k + 1],
                                     bias=cols[:, LN_B + k:LN_B + k + 1]).then_inc(operand_ready, 1)
                act.wait_ge(operand_ready, KT * LN_NORM + k + 1)
                nc.scalar.activation(h_hi[:, k], wide[:, k, PAD:PAD + L], ACT.Copy).then_inc(h_hi_ready, 1)
            hi_d(DC + 2)
            hi_g(G0[3] + 1)
            hi_d(DC + 3)
            hi_u(U0[3] + 1)
            hi_d(D0[3])
            stage(5)

            middle(3)
            block_out(3, NB - 2)
            hi_d(D0[3] + NB - 1)
            block_out(3, NB - 1)
            stage(6, hi=False)
            for n in (1, 3):
                act.wait_ge(out_psum, n + 1)
                nc.scalar.activation(out_rows[:, n % 2, n // 2 * 512:n // 2 * 512 + 512], ps_d[:, n], ACT.Copy).then_inc(out_ready[1], 1)

        @block.vector
        def _(dve):
            def lo_g(n, i=0):
                dve.wait_ge(s_g_hi, n + 1 + 2 * i)
                dve.tensor_tensor(g_lo[:, n % 2], g_raw[:, n % 2], f32(g_hi[:, n % 2]), ALU.subtract).then_inc(s_g_lo, 1)

            def lo_u(n, i=0):
                dve.wait_ge(s_u_hi, n + 1 + 2 * i)
                dve.tensor_tensor(u_lo[:, n % 2], u_raw[:, n % 2], f32(u_hi[:, n % 2]), ALU.subtract).then_inc(s_u_lo, 1)

            def lo_d(n, i=0):
                dve.wait_ge(s_d_hi, n + 1 + 2 * i)
                dve.tensor_tensor(d_lo[:, n % 2], d_raw[:], f32(d_hi[:, n % 2]), ALU.subtract).then_inc(s_d_lo, 1)

            def mod_acc(v, i=0):
                raw = {1: g_raw, 2: u_raw}.get(v, m_raw)
                arrived = {1: g_in, 2: u_in}.get(v, m_in)
                if v >= 1:
                    dve.wait_ge(reduced, v + 2 * i)
                for k in range(KT):
                    if k % 4 == 0:
                        h = k // 4
                        w = raw[:, h].rearrange("p k n -> p (k n)")
                        dve.wait_ge(arrived[h], (16 * (v - 1) if v >= 3 else 16) + 32 * i)
                    wk = w[:, (k % 4) * MOD_COLS:(k % 4 + 1) * MOD_COLS]
                    if k == 0:
                        dve.tensor_scalar(acc[:], wk, csilu[:, 0:1], None, ALU.mult).then_inc(acc_step, 1)
                    else:
                        dve.wait_ge(acc_step, 8 * v + k + 16 * i)
                        dve.scalar_tensor_tensor(out=acc[:], in0=wk, scalar=csilu[:, k:k + 1], in1=acc[:],
                                                 op0=ALU.mult, op1=ALU.add).then_inc(acc_step, 1)

            def mod_out(v, i=0):
                dve.wait_ge(reduced, v + 1 + 2 * i)
                dve.tensor_tensor(mcol[:, bass.ds(v * MOD_SUB + i * (2 * MOD_SUB), MOD_SUB)], ps_mod[:, 0:MOD_SUB],
                                  cols[:, bass.ds(MOD_B + v * MOD_SUB + i * (2 * MOD_SUB), MOD_SUB)],
                                  ALU.add).then_inc(mcol_ready, 1)

            def block_out(f, b, i=0):
                e = NB * f + b
                dve.wait_ge(gated_ready, e + 1 + 2 * i)
                if e >= 1:
                    dve.wait_ge(a_lo_ready, e + 2 * i)
                dve.tensor_tensor(prod, gated, ps_u[:], ALU.mult).then_inc(prod_ready, 1)
                dve.wait_ge(a_hi_ready, e + 1 + 2 * i)
                dve.tensor_tensor(a_lo[:, b % 2].rearrange("p j t -> p (j t)"), prod,
                                  f32(a_hi[:, b % 2].rearrange("p j t -> p (j t)")), ALU.subtract).then_inc(a_lo_ready, 1)

            def mods(f, b, i=0):
                if MOD_PRE[f] is not None and b - 1 <= MOD_LAST[f]:
                    mod_out(MOD_AT[f] + b - 1 if b else MOD_PRE[f], i)

            def steady(f, b, i=0):
                block_out(f, b, i)
                mods(f, b, i)
                lo_g(G0[f] + b + 2, i)
                lo_u(U0[f] + b + 2, i)
                lo_d(D0[f] + b + 1, i)
                if b <= MOD_LAST[f]:
                    mod_acc(MOD_AT[f] + b, i)

            def middle(f):
                steady(f, 0)
                with dve.Fori(0, LOOPS) as i:
                    steady(f, 1, i)
                    steady(f, 2, i)

            def norm_coef(s, layer, k):
                g = NORM_G + (layer * 3 + k) * KT
                m = mod_at(layer, 3 * k + 1)
                dve.scalar_tensor_tensor(out=coef[:], in0=mcol[:, m:m + KT], scalar=1.0, in1=cols[:, g:g + KT],
                                         op0=ALU.add, op1=ALU.mult).then_inc(coef_ready, 1)

            def residual(s, wait, gate):
                for q in range(PAIRS):
                    dve.wait_ge(*wait(q))
                    for k in (2 * q, 2 * q + 1):
                        ins = dve.scalar_tensor_tensor(out=xs[:, k], in0=ps_d[:, q, (k % 2) * L:(k % 2 + 1) * L],
                                                       scalar=gate[:, k:k + 1], in1=xs[:, k], op0=ALU.mult, op1=ALU.add)
                    ins.then_inc(x_ready, 1)

            def norm_rstd(r):
                dve.wait_ge(root_ready, r + 1)
                dve.reciprocal(rstd, root).then_inc(rstd_ready, 1)
                dve.wait_ge(rstd_ready, r + 1)

            def scale_tile(r, k, source):
                if k >= 2:
                    if r == 1:
                        dve.wait_ge(pool_step, k - 1)
                    else:
                        dve.wait_ge(operand_ready, KT * r + k - 1)
                dve.tensor_tensor(scaled[k % 2], source[:, k], rstd, ALU.mult).then_inc(scaled_ready, 1)

            def norm_tiles(r, shift):
                scale_tile(r, 0, xs)
                for k in range(KT):
                    if k + 1 < KT:
                        scale_tile(r, k + 1, xs)
                    dve.wait_ge(scaled_ready, KT * r + k + 1)
                    ins = dve.tensor_scalar(wide[:, k, PAD:PAD + L], scaled[k % 2], coef[:, k:k + 1],
                                            shift[:, k:k + 1], ALU.mult, ALU.add)
                    if r == 1:
                        ins.then_inc(pool_step, 1)
                    else:
                        ins.then_inc(operand_ready, 1)
                        if k >= 1:
                            norm_lo(r, k - 1)
                if r != 1:
                    norm_lo(r, KT - 1)

            def norm_lo(r, k):
                dve.wait_ge(h_hi_ready, KT * r + k + 1)
                dve.tensor_tensor(h_lo[:, k], wide[:, k, PAD:PAD + L], f32(h_hi[:, k]), ALU.subtract).then_inc(h_lo_ready, 1)

            def stage_norm(s, layer, k):
                r = NORM_OF_STAGE[s]
                norm_rstd(r)
                m = mod_at(layer, 3 * k)
                norm_tiles(r, mcol[:, m:m + KT])

            def half_gate(layer, k):
                m = mod_at(layer, 3 * k + 2)
                dve.tensor_scalar(gcoef[:], mcol[:, m:m + KT], 0.5, None, ALU.mult).then_inc(coef_ready, 1)

            def ffn_bank(f):
                k = [0, 2, 3, 5][f]
                return lambda q: (bank_ready, 3 * k + q + 1) if q < PAIRS - 1 else (d_done, D0[f] + NB)

            dve.wait_ge(cols_psum, 1)
            dve.tensor_copy(cols[:], ps_u[:, 0:N_COLS]).then_inc(cols_ready, 1)
            for q in range(PAIRS):
                dve.wait_ge(xt_ready, q + 1)
                dve.tensor_copy(xs[:, 2 * q:2 * q + 2].rearrange("p k t -> p (k t)"), ps_d[:, q]).then_inc(x_ready, 1)
            dve.wait_ge(consts_ready, CONSTS)
            dve.reciprocal(edge[:], edge[:]).then_inc(edge_step, 1)
            dve.wait_ge(edge_step, 1)
            for g, w in enumerate(POOL_WINDOWS):
                dve.tensor_scalar(edge[:, g], edge[:, g], float(w), None, ALU.mult).then_inc(edge_step, 1)
            dve.wait_ge(csilu_ready, 1)
            for v in range(4):
                mod_acc(v)
                mod_out(v)
            dve.wait_ge(mcol_ready, 4)
            norm_coef(0, 0, 0)
            dve.wait_ge(coef_ready, 1)
            stage_norm(0, 0, 0)
            lo_g(0)
            lo_g(1)
            lo_u(0)
            lo_u(1)
            lo_d(0)
            mod_acc(MOD_PRE[0])

            middle(0)
            block_out(0, NB - 2)
            mods(0, NB - 2)
            lo_g(NB)
            lo_u(NB)
            lo_d(NB - 1)
            mod_acc(MOD_AT[0] + NB - 2)
            block_out(0, NB - 1)
            mods(0, NB - 1)
            mod_acc(MOD_AT[0] + NB - 1)
            lo_g(NB + 1)
            dve.wait_ge(mcol_ready, 15)
            norm_coef(1, 0, 1)
            half_gate(0, 0)
            dve.wait_ge(coef_ready, 3)
            residual(1, ffn_bank(0), gcoef)
            mod_out(MOD_AT[0] + NB - 1)
            stage_norm(1, 0, 1)
            dve.wait_ge(edge_step, 1 + len(POOL_WINDOWS))
            steps = KT
            for g, w in enumerate(POOL_WINDOWS):
                dve.wait_ge(pool_step, steps)
                if g >= 1:
                    dve.wait_ge(operand_ready, KT + 2 * g)
                ks = slice(2 * g, 2 * g + 2)
                first = PAD - w // 2
                n = L + w - 2
                cur = wide[:, ks, first:first + n + 1]
                half = 1
                turn = 0
                while half < w:
                    n = L + w - 2 * half
                    dst = run_sum[turn][:, :, 0:n]
                    dve.tensor_tensor(dst, cur[:, :, 0:n], cur[:, :, half:half + n], ALU.add).then_inc(pool_step, 1)
                    steps += 1
                    dve.wait_ge(pool_step, steps)
                    cur, half, turn = run_sum[turn], 2 * half, 1 - turn
                for e, at in enumerate((0, L - w // 2)):
                    piece = cur[:, :, at:at + w // 2]
                    dve.tensor_tensor(piece, piece, edge[:, g, e, 0:w // 2].unsqueeze(1).to_broadcast([P, 2, w // 2]),
                                      ALU.mult).then_inc(pool_step, 1)
                    steps += 1
                dve.wait_ge(pool_step, steps)
                for k in (0, 1):
                    own = wide[:, 2 * g + k, PAD:PAD + L]
                    dve.scalar_tensor_tensor(out=own, in0=cur[:, k, 0:L], scalar=1.0 / w, in1=own,
                                             op0=ALU.mult, op1=ALU.subtract).then_inc(operand_ready, 1)
                if g >= 1:
                    norm_lo(1, 2 * g - 2)
                    norm_lo(1, 2 * g - 1)
            norm_lo(1, KT - 2)
            norm_lo(1, KT - 1)
            lo_u(NB + 1)
            m = mod_at(0, 5)
            dve.tensor_tensor(gcoef[:], mcol[:, m:m + KT], cols[:, POOL_SC:POOL_SC + KT], ALU.mult).then_inc(coef_ready, 1)
            dve.wait_ge(mcol_ready, 16)
            norm_coef(2, 0, 2)
            dve.wait_ge(coef_ready, 5)
            residual(2, lambda q: (bank_ready, 3 + q + 1) if q < PAIRS - 1 else (gu_done, NB + 1), gcoef)
            stage_norm(2, 0, 2)
            mod_acc(MOD_PRE[1])
            lo_d(NB)
            lo_g(NB + 2)

            middle(1)
            for b in (NB - 2, NB - 1):
                steady(1, b)
            dve.wait_ge(mcol_ready, 26)
            norm_coef(3, 1, 0)
            half_gate(0, 2)
            dve.wait_ge(coef_ready, 7)
            residual(3, ffn_bank(1), gcoef)
            stage_norm(3, 1, 0)
            mod_acc(MOD_PRE[2])

            middle(2)
            for b in (NB - 2, NB - 1):
                steady(2, b)
            dve.wait_ge(mcol_ready, 36)
            norm_coef(4, 1, 1)
            half_gate(1, 0)
            dve.wait_ge(coef_ready, 9)
            residual(4, ffn_bank(2), gcoef)
            stage_norm(4, 1, 1)

            def glu(b):
                dve.wait_ge(glu_gate_ready, b + 1)
                src = ps_g if b % 2 == 0 else ps_d[:, 0]
                for k in (0, 1):
                    dve.tensor_tensor(wide[:, 2 * b + k, PAD:PAD + L], gated[:, k * L:(k + 1) * L],
                                      src[:, k * L:(k + 1) * L], ALU.mult).then_inc(glu_ready, 1)

            taps_done = [0]

            def taps(tiles):
                dve.wait_ge(glu_ready, max(tiles) + 1)
                for w in range(TAPS):
                    for n, k in enumerate(tiles):
                        col = cols[:, DW + w * KT + k:DW + w * KT + k + 1]
                        src = wide[:, k, w:w + L]
                        if w == 0:
                            dve.tensor_scalar(conv[:, k], src, col, None, ALU.mult).then_inc(tap_step, 1)
                        else:
                            dve.wait_ge(tap_step, taps_done[0] - len(tiles) + 1)
                            dve.scalar_tensor_tensor(out=conv[:, k], in0=src, scalar=col, in1=conv[:, k],
                                                     op0=ALU.mult, op1=ALU.add).then_inc(tap_step, 1)
                        taps_done[0] += 1

            glu(0)
            lo_g(GC + 2)
            lo_u(UC + 2)
            taps((0,))
            glu(1)
            lo_g(GC + 3)
            lo_u(UC + 3)
            taps((1,))
            glu(2)
            lo_d(DC + 1)
            glu(3)
            taps((2, 3, 4))
            for k in CONV_TILES_ON_PE:
                dve.wait_ge(diag_used, TAPS * (CONV_TILES_ON_PE.index(k) + 1))
                dve.tensor_copy(conv[:, k], ps_d[:, CONV_BANK[k], 0:L]).then_inc(conv_ready, 1)
            dve.wait_ge(mu_ready, 1)
            for q in range(PAIRS):
                dve.tensor_tensor(conv[:, 2 * q:2 * q + 2], conv[:, 2 * q:2 * q + 2],
                                  ps_mod[:, 0:L].unsqueeze(1).to_broadcast([P, 2, L]), ALU.subtract).then_inc(centred, 1)
            norm_rstd(LN_NORM)
            for k in range(KT):
                scale_tile(LN_NORM, k, conv)
                if k >= 1:
                    norm_lo(LN_NORM, k - 1)
            norm_lo(LN_NORM, KT - 1)
            lo_g(G0[3])
            lo_u(U0[3])
            lo_d(DC + 2)
            lo_g(G0[3] + 1)
            lo_d(DC + 3)
            lo_u(U0[3] + 1)
            lo_d(D0[3])
            norm_coef(5, 1, 2)
            dve.wait_ge(coef_ready, 10)
            m = mod_at(1, 5)
            residual(5, lambda q: (bank_ready, 3 * 4 + q + 1) if q < PAIRS - 1 else (d_done, DC + NC), mcol[:, m:m + KT])
            stage_norm(5, 1, 2)

            middle(3)
            block_out(3, NB - 2)
            lo_d(D0[3] + NB - 1)
            block_out(3, NB - 1)
            half_gate(1, 2)
            dve.wait_ge(coef_ready, 11)
            residual(6, ffn_bank(3), gcoef)
            r = NORM_OF_STAGE[6]
            norm_rstd(r)
            scale_tile(r, 0, xs)
            for k in range(KT):
                if k + 1 < KT:
                    scale_tile(r, k + 1, xs)
                dve.wait_ge(scaled_ready, KT * r + k + 1)
                dve.tensor_scalar(wide[:, k, PAD:PAD + L], scaled[k % 2], cols[:, FINAL_G + k:FINAL_G + k + 1],
                                  None, ALU.mult).then_inc(operand_ready, 1)
            for n in (0, 2):
                dve.wait_ge(out_psum, n + 1)
                dve.tensor_copy(out_rows[:, n % 2, n // 2 * 512:n // 2 * 512 + 512], ps_d[:, n]).then_inc(out_ready[0], 1)

        @block.tensor
        def _(pe):
            def mm3(dst, w_hi, w_lo, m_hi, m_lo, start, stop):
                pe.matmul(dst, w_hi, m_hi, start=start, stop=False, skip_group_check=True)
                pe.matmul(dst, w_hi, m_lo, start=False, stop=False, skip_group_check=True)
                return pe.matmul(dst, w_lo, m_hi, start=False, stop=stop, skip_group_check=True)

            def gate_up(g, u, lo_from, i=0, banks=None):
                pe.wait_ge(s_g_lo, g + 1 + 2 * i)
                pe.wait_ge(s_u_lo, u + 1 + 2 * i)
                dst_g, dst_u = banks or (ps_g, ps_u)
                for k in range(KT):
                    if lo_from is not None:
                        pe.wait_ge(h_lo_ready, lo_from + k + 1)
                    for dst, hi, lo, slot in ((dst_g, g_hi, g_lo, g % 2), (dst_u, u_hi, u_lo, u % 2)):
                        for j in range(SUB):
                            mm = mm3(dst[:, j * L:(j + 1) * L], hi[:, slot, k, j * P:(j + 1) * P],
                                     lo[:, slot, k, j * P:(j + 1) * P], h_hi[:, k], h_lo[:, k],
                                     start=(k == 0 and j == 0), stop=(k == KT - 1))
                mm.then_inc(gu_done, 1)

            def ffn_block(f, b, i=0):
                e = NB * f + b
                if e >= 1:
                    pe.wait_ge(prod_ready, e + 2 * i)
                gate_up(G0[f] + b, U0[f] + b, KT * NORM_OF_STAGE[FFN_STAGE[f]] if b == 0 else None, i)

            def mod_reduce(v, i=0):
                pe.wait_ge(acc_step, 8 * (v + 1) + 16 * i)
                if v >= 1:
                    pe.wait_ge(mcol_ready, v + 2 * i)
                for j in range(MOD_SUB):
                    mm = pe.matmul(ps_mod[:, j:j + 1], acc[:, j * P:(j + 1) * P], one[:], start=True, stop=True,
                                   skip_group_check=True)
                mm.then_inc(reduced, 1)

            def down_unit(d, first, m_hi, m_lo, tiles, i=0, stop=False):
                for j in range(SUB):
                    for k in tiles:
                        mm = mm3(ps_d[:, k // 2, (k % 2) * L:(k % 2 + 1) * L], d_hi[:, d % 2, j, k * P:(k + 1) * P],
                                 d_lo[:, d % 2, j, k * P:(k + 1) * P], m_hi(j), m_lo(j),
                                 start=(first and j == 0 and k % 2 == 0), stop=(stop and j == SUB - 1))
                return mm

            def last_down(d, m_hi, m_lo):
                for q in range(PAIRS):
                    mm = down_unit(d, False, m_hi, m_lo, (2 * q, 2 * q + 1), stop=True)
                    mm.then_inc(bank_ready if q < PAIRS - 1 else d_done, 1)

            def ffn_down(f, b, i=0):
                d = D0[f] + b
                pe.wait_ge(s_d_lo, d + 1 + 2 * i)
                pe.wait_ge(a_lo_ready, NB * f + b + 1 + 2 * i)
                m_hi, m_lo = (lambda j: a_hi[:, b % 2, j]), (lambda j: a_lo[:, b % 2, j])
                if b == NB - 1:
                    last_down(d, m_hi, m_lo)
                else:
                    down_unit(d, b == 0, m_hi, m_lo, range(KT), i).then_inc(d_done, 1)

            def steady(f, b, i=0):
                ffn_block(f, b, i)
                if b - 1 <= MOD_LAST[f]:
                    mod_reduce(MOD_AT[f] + b - 1, i)
                ffn_down(f, b - 1, i)

            def ffn(f):
                ffn_block(f, 0)
                if MOD_PRE[f] is not None:
                    mod_reduce(MOD_PRE[f])
                steady(f, 1)
                with pe.Fori(0, LOOPS) as i:
                    steady(f, 2, i)
                    steady(f, 3, i)
                steady(f, NB - 1)
                ffn_down(f, NB - 1)

            def stat(r):
                for q in range(PAIRS):
                    pe.wait_ge(sq_ready, PAIRS * r + q + 1)
                    for k in (0, 1):
                        mm = pe.matmul(ps_stat[:, 0:L], mean_w[:], sq[q % 2][:, k * L:(k + 1) * L],
                                       start=(q == 0 and k == 0), stop=(q == PAIRS - 1 and k == 1), skip_group_check=True)
                    mm.then_inc(stat_step, 1)

            pe.wait_ge(consts_ready, 3)
            pe.wait_ge(vec_in, 16 * VEC_LOADS)
            at = 0
            for r, n in enumerate((MOD_B, N_MOD * KT, N_MOD * KT, TAPS * KT // 2, TAPS * KT // 2)):
                mm = pe.transpose(ps_u[:, at:at + n], vec_rows[0:n, r, :], ident[0:n, 0:n])
                at += n
            mm.then_inc(cols_psum, 1)
            pe.wait_ge(x_in, 16)
            for q in range(PAIRS):
                for k in (0, 1):
                    for a in range(L // P):
                        mm = pe.transpose(ps_d[:, q, k * L + a * P:k * L + (a + 1) * P],
                                          x_rows[:, a, (2 * q + k) * P:(2 * q + k + 1) * P], ident[:])
                mm.then_inc(xt_ready, 1)
            stat(0)
            for v in range(4):
                mod_reduce(v)

            ffn(0)
            mod_reduce(MOD_AT[0] + NB - 1)
            stat(1)
            pe.wait_ge(s_g_lo, NB + 1)
            slot = NB % 2
            for g in range(len(POOL_WINDOWS)):
                pe.wait_ge(h_lo_ready, KT * 1 + 2 * g + 2)
                for m in range(SUB):
                    for j in range(SUB):
                        mm = mm3(ps_d[:, g, m * L:(m + 1) * L], g_hi[:, slot, 2 * g + j, m * P:(m + 1) * P],
                                 g_lo[:, slot, 2 * g + j, m * P:(m + 1) * P], h_hi[:, 2 * g + j], h_lo[:, 2 * g + j],
                                 start=(m == 0 and j == 0), stop=(j == SUB - 1))
                mm.then_inc(bank_ready if g < PAIRS - 1 else gu_done, 1)
            stat(2)

            for f in (1, 2):
                ffn(f)
                stat(NORM_OF_STAGE[f + 2])

            for b in range(NC):
                if b >= 2:
                    pe.wait_ge(glu_ready, 2 * (b - 1))
                gate_up(GC + b, UC + b, KT * 4 if b == 0 else None, banks=None if b % 2 == 0 else (ps_d[:, 0], ps_d[:, 1]))
            n = 0
            for t in CONV_TILES_ON_PE:
                pe.wait_ge(glu_ready, t + 1)
                for w in range(TAPS):
                    pe.wait_ge(diag_ready, n + 1)
                    mm = pe.matmul(ps_d[:, CONV_BANK[t], 0:L], diag[:, n % DIAG_SLOTS], wide[:, t, w:w + L],
                                   start=(w == 0), stop=(w == TAPS - 1), skip_group_check=True)
                    mm.then_inc(diag_used, 1)
                    n += 1
            pe.wait_ge(tap_step, TAPS * (KT - len(CONV_TILES_ON_PE)))
            pe.wait_ge(conv_ready, len(CONV_TILES_ON_PE))
            for k in range(KT):
                mm = pe.matmul(ps_mod[:, 0:L], mean_w[:], conv[:, k], start=(k == 0), stop=(k == KT - 1), skip_group_check=True)
            mm.then_inc(mu_ready, 1)
            stat(LN_NORM)
            for b in range(NC):
                pe.wait_ge(s_d_lo, DC + b + 1)
                if b == 0:
                    pe.wait_ge(h_lo_ready, KT * (LN_NORM + 1))
                m_hi, m_lo = (lambda j: h_hi[:, 2 * b + j]), (lambda j: h_lo[:, 2 * b + j])
                if b == NC - 1:
                    last_down(DC + b, m_hi, m_lo)
                else:
                    down_unit(DC + b, b == 0, m_hi, m_lo, range(KT)).then_inc(d_done, 1)
            stat(NORM_OF_STAGE[5])

            ffn(3)
            r = NORM_OF_STAGE[6]
            stat(r)
            for n in range(PAIRS):
                a, half = n % 2, n // 2
                for k in range(KT // 2):
                    dt = half * (KT // 2) + k
                    pe.wait_ge(operand_ready, KT * r + dt + 1)
                    mm = pe.transpose(ps_d[:, n, k * P:(k + 1) * P], wide[:, dt, PAD + a * P:PAD + (a + 1) * P], ident[:])
                mm.then_inc(out_psum, 1)


_INS = ['x', 'c', 'mod_w', 'mod_b', 'norm_g', 'final_g', 'ffn_w_gate', 'ffn_w_up', 'ffn_w_down', 'pool_w',
        'pool_scale', 'conv_w_in', 'conv_dw', 'conv_ln_g', 'conv_ln_b', 'conv_w_out']


def kernel(**inputs):
    import numpy as _np
    import concourse.bacc as _bacc
    from concourse import mybir as _mybir
    from concourse.bass_utils import run_bass_kernel_spmd as _run

    nc = _bacc.Bacc("TRN2", target_bir_lowering=False, num_devices=1)
    arrays, args = {}, []
    for name in _INS:
        a = _np.ascontiguousarray(inputs[name])
        arrays[f"in_{name}_dram"] = a
        args.append(nc.dram_tensor(f"in_{name}_dram", a.shape, _mybir.dt.from_np(a.dtype), kind="ExternalInput").ap())
    x = inputs['x']
    out = nc.dram_tensor("out_0_dram", x.shape, _mybir.dt.from_np(_np.dtype(x.dtype)), kind="ExternalOutput").ap()
    backbone_kernel(nc, *args, out)
    r = _run(nc, [arrays], core_ids=[0])
    return r.results[0]["out_0_dram"]
```

```python
from contextlib import ExitStack

import concourse.bass as bass
from concourse import mybir

ALU = mybir.AluOpType
ACT = mybir.ActivationFunctionType
F32 = mybir.dt.float32
F32R = mybir.dt.float32r

P = 128
EPS = 1e-6
POOL_WINDOWS = (2, 4, 8, 16)
PAD = 15
MOD_COLS = 512
BLK = 256
SUB = BLK // P
DIAG_SLOTS = 8
CONV_TILES_ON_PE = (5, 6, 7)


def backbone_kernel(nc, x, c, mod_w, mod_b, norm_g, final_g, ffn_w_gate, ffn_w_up, ffn_w_down,
                    pool_w, pool_scale, conv_w_in, conv_dw, conv_ln_g, conv_ln_b, conv_w_out, out):
    _, L, D = x.shape
    DEPTH, _, _, FF = ffn_w_gate.shape
    TAPS = conv_dw.shape[1]
    KT = D // P
    NB = FF // BLK
    NC = D // BLK
    PAIRS = KT // 2
    N_MOD = mod_w.shape[2] // D
    MOD_UNITS = N_MOD * D // MOD_COLS
    MOD_SUB = MOD_COLS // P
    WIDTH = L + 2 * PAD
    LOOPS = (NB - 3) // 2
    assert DEPTH == 2 and L == 256 and KT == 8 and NB == 11 and NC == 4 and TAPS == 2 * PAD + 1
    assert MOD_UNITS == 18

    G0 = [0, NB + 1, 2 * NB + 1, 3 * NB + 1 + NC]
    U0 = [0, NB, 2 * NB, 3 * NB + NC]
    D0 = [0, NB, 2 * NB, 3 * NB + NC]
    GC, UC, DC = 3 * NB + 1, 3 * NB, 3 * NB
    MOD_PRE = [4, 16, 26, None]
    MOD_AT = [5, 17, 27, None]
    MOD_LAST = [NB - 1, NB - 3, NB - 3, -1]
    D_LAST = D0[3] + NB - 2

    NORM_G, FINAL_G = 0, DEPTH * 3 * KT
    POOL_SC, LN_G, LN_B, C_COL = (FINAL_G + (j + 1) * KT for j in range(4))
    MOD_B = C_COL + KT
    DW = MOD_B + DEPTH * N_MOD * KT
    N_COLS = DW + TAPS * KT

    with ExitStack() as ctx:
        def sb(name, shape, dt=F32):
            return ctx.enter_context(nc.sbuf_tensor(name, shape, dt))

        def psum(name, shape):
            return ctx.enter_context(nc.psum_tensor(name, shape, F32))

        def sem(name):
            return ctx.enter_context(nc.semaphore(name))

        g_raw, u_raw = sb("g_raw", [P, 2, KT, BLK]), sb("u_raw", [P, 2, KT, BLK])
        d_raw = sb("d_raw", [P, 2, SUB, D])
        g_hi, g_lo = sb("g_hi", [P, 2, KT, BLK], F32R), sb("g_lo", [P, 2, KT, BLK], F32R)
        u_hi, u_lo = sb("u_hi", [P, 2, KT, BLK], F32R), sb("u_lo", [P, 2, KT, BLK], F32R)
        d_hi, d_lo = sb("d_hi", [P, 2, SUB, D], F32R), sb("d_lo", [P, 2, SUB, D], F32R)
        m_raw = sb("m_raw", [P, 2, KT // 2, MOD_COLS])
        xs = sb("xs", [P, KT, L])
        wide = sb("wide", [P, KT, WIDTH])
        h_hi, h_lo = sb("h_hi", [P, KT, L], F32R), sb("h_lo", [P, KT, L], F32R)
        a_hi, a_lo = sb("a_hi", [P, 2, SUB, L], F32R), sb("a_lo", [P, 2, SUB, L], F32R)
        scr = sb("scr", [P, 2048])
        cols = sb("cols", [P, N_COLS])
        mcol = sb("mcol", [P, DEPTH * N_MOD * KT])
        acc = sb("acc", [P, 2, MOD_COLS])
        csilu = sb("csilu", [P, KT])
        coef = sb("coef", [P, KT])
        gcoef = sb("gcoef", [P, KT])
        edge = sb("edge", [P, len(POOL_WINDOWS), 2, max(POOL_WINDOWS) // 2])
        eps = sb("eps", [P, 1])
        one = sb("one", [P, 1])
        mean_w = sb("mean_w", [P, P])
        ident = sb("ident", [P, P])

        x_rows = d_raw[:, 1]
        out_rows = d_raw[:, D_LAST % 2]
        conv = m_raw[:].rearrange("p a k n -> p (a k n)")[:, 0:KT * L].rearrange("p (k t) -> p k t", k=KT)
        vec_rows = scr[:, 0:5 * P].rearrange("p (r n) -> p r n", r=5)
        gated = scr[:, 0:512]
        prod = scr[:, 512:1024]
        sq = [scr[:, 512 * j:512 * (j + 1)] for j in range(2)]
        root, rstd = scr[:, 1024:1280], scr[:, 1280:1536]
        scaled = [scr[:, 1536 + 256 * j:1792 + 256 * j] for j in range(2)]
        run_sum = [scr[:, 544 * j:544 * (j + 1)].rearrange("p (k t) -> p k t", k=2) for j in range(2)]
        diag = scr[:, 1024:1024 + DIAG_SLOTS * P].rearrange("p (s n) -> p s n", s=DIAG_SLOTS)

        ps_g, ps_u, ps_mod, ps_stat = (psum(n, [P, 512]) for n in ("ps_g", "ps_u", "ps_mod", "ps_stat"))
        ps_d = psum("ps_d", [P, PAIRS, 512])
        CONV_BANK = dict(zip(CONV_TILES_ON_PE, (3, 2, 0)))

        vec_in, stored = sem("vec_in"), sem("stored")
        g_in, u_in = [sem("g_in0"), sem("g_in1")], [sem("u_in0"), sem("u_in1")]
        m_in, d_in = [sem("m_in0"), sem("m_in1")], [sem("d_in0"), sem("d_in1")]
        s_g_hi, s_g_lo, s_u_hi, s_u_lo = sem("g_hi_ready"), sem("g_lo_ready"), sem("u_hi_ready"), sem("u_lo_ready")
        s_d_hi, s_d_lo = sem("d_hi_ready"), sem("d_lo_ready")
        gu_done, d_done = sem("gu_done"), sem("d_done")
        acc_step, reduced, mcol_ready = sem("acc_step"), sem("reduced"), sem("mcol_ready")
        gated_ready, prod_ready, a_hi_ready, a_lo_ready = (
            sem("gated_ready"), sem("prod_ready"), sem("a_hi_ready"), sem("a_lo_ready"))
        bank_ready, x_ready, sq_ready, stat_step = sem("bank_ready"), sem("x_ready"), sem("sq_ready"), sem("stat_step")
        root_ready, rstd_ready, coef_ready = sem("root_ready"), sem("rstd_ready"), sem("coef_ready")
        scaled_ready, operand_ready, h_hi_ready, h_lo_ready = (
            sem("scaled_ready"), sem("operand_ready"), sem("h_hi_ready"), sem("h_lo_ready"))
        consts_ready, consts_step, xt_ready, cols_psum, cols_ready, csilu_ready = (
            sem("consts_ready"), sem("consts_step"), sem("xt_ready"), sem("cols_psum"),
            sem("cols_ready"), sem("csilu_ready"))
        edge_step, pool_in, pool_step = sem("edge_step"), sem("pool_in"), sem("pool_step")
        glu_gate_ready, glu_ready, tap_step, diag_ready, diag_used, conv_ready = (
            sem("glu_gate_ready"), sem("glu_ready"), sem("tap_step"), sem("diag_ready"), sem("diag_used"),
            sem("conv_ready"))
        mu_ready, centred = sem("mu_ready"), sem("centred")
        out_psum, out_ready = sem("out_psum"), [sem("out_ready_dve"), sem("out_ready_act")]

        gate_v = ffn_w_gate.rearrange("l f (k p) n -> l f p k n", p=P)
        up_v = ffn_w_up.rearrange("l f (k p) n -> l f p k n", p=P)
        down_v = ffn_w_down.rearrange("l f (j p) n -> l f p j n", p=P)
        mod_v = mod_w.rearrange("l (k p) n -> l p k n", p=P)
        conv_in_v = conv_w_in.rearrange("l (k p) n -> l p k n", p=P)
        conv_out_v = conv_w_out.rearrange("l (j p) n -> l p j n", p=P)
        pool_v = pool_w.rearrange("l g (j p) n -> l p (g j) n", p=P)
        x_v = x.rearrange("b (a p) d -> (b p) a d", p=P)
        out_v = out.rearrange("b (a p) d -> (b p) a d", p=P)

        NORM_OF_STAGE = [0, 1, 2, 3, 4, 6, 7]
        LN_NORM = 5
        FFN_STAGE = [0, 2, 3, 5]
        FFN_LAYER = [0, 0, 1, 1]

        CONSTS = 4 + 2 * len(POOL_WINDOWS) + 1

        half_dw = TAPS * KT // 2
        dw_rows = conv_dw.rearrange("l w (k n) -> (l w k) n", n=P)
        vec_loads = [
            (vec_rows[NORM_G:FINAL_G, 0], norm_g.rearrange("l r (k n) -> (l r k) n", n=P)),
            (vec_rows[FINAL_G:POOL_SC, 0], final_g.rearrange("(k n) -> k n", n=P)),
            (vec_rows[POOL_SC:LN_G, 0], pool_scale.rearrange("l (k n) -> (l k) n", n=P)),
            (vec_rows[LN_G:LN_B, 0], conv_ln_g.rearrange("l (k n) -> (l k) n", n=P)),
            (vec_rows[LN_B:C_COL, 0], conv_ln_b.rearrange("l (k n) -> (l k) n", n=P)),
            (vec_rows[C_COL:MOD_B, 0], c.rearrange("b (k n) -> (b k) n", n=P)),
        ]
        for j in range(2):
            vec_loads.append((vec_rows[0:N_MOD * KT, 1 + j], mod_b[j].rearrange("(k n) -> k n", n=P)))
            vec_loads.append((vec_rows[0:half_dw, 3 + j], dw_rows[j * half_dw:(j + 1) * half_dw]))
        VEC_LOADS = len(vec_loads)

        def mod_at(layer, k):
            return (layer * N_MOD + k) * KT

        def f32(ap):
            return ap.bitcast(F32)

        block = ctx.enter_context(nc.Block())

        @block.sync
        def _(sp):
            def load_g(n, i, src):
                if n >= 2:
                    sp.wait_ge(s_g_lo, n - 1 + 2 * i)
                else:
                    sp.wait_ge(acc_step, 4 * (3 + n))
                sp.dma_start(g_raw[:, n % 2], src).then_inc(g_in[n % 2], 16)

            def load_u(n, i, src):
                if n >= 2:
                    sp.wait_ge(s_u_lo, n - 1 + 2 * i)
                else:
                    sp.wait_ge(acc_step, 4 * (5 + n))
                sp.dma_start(u_raw[:, n % 2], src).then_inc(u_in[n % 2], 16)

            def load_d(n, i, src):
                if n >= 2:
                    sp.wait_ge(s_d_lo, n - 1 + 2 * i)
                elif n == 1:
                    sp.wait_ge(xt_ready, PAIRS)
                sp.dma_start(d_raw[:, n % 2], src).then_inc(d_in[n % 2], 16)

            def load_mod(v, i):
                layer = v // MOD_UNITS
                for h in range(2):
                    src = mod_v[layer, :, 4 * h:4 * h + 4, bass.ds((v - layer * MOD_UNITS) * MOD_COLS + i * (2 * MOD_COLS), MOD_COLS)]
                    if v == 1:
                        sp.dma_start(g_raw[:, h].rearrange("p k n -> p (k n)").rearrange("p (k n) -> p k n", n=MOD_COLS), src).then_inc(g_in[h], 16)
                    elif v == 2:
                        sp.dma_start(u_raw[:, h].rearrange("p k n -> p (k n)").rearrange("p (k n) -> p k n", n=MOD_COLS), src).then_inc(u_in[h], 16)
                    else:
                        if v == 3:
                            sp.wait_ge(acc_step, 4 * (h + 1))
                        elif v >= 4:
                            sp.wait_ge(acc_step, 8 * v + 4 * h - 4 + 16 * i)
                        sp.dma_start(m_raw[:, h], src).then_inc(m_in[h], 16)

            def ffn_g(f, b, i=0):
                load_g(G0[f] + b, i, gate_v[FFN_LAYER[f], f % 2, :, :, bass.ds(b * BLK + i * (2 * BLK), BLK)])

            def ffn_u(f, b, i=0):
                load_u(U0[f] + b, i, up_v[FFN_LAYER[f], f % 2, :, :, bass.ds(b * BLK + i * (2 * BLK), BLK)])

            def ffn_d(f, b, i=0):
                load_d(D0[f] + b, i, down_v[FFN_LAYER[f], f % 2, :, bass.ds(b * SUB + i * (2 * SUB), SUB), :])

            def conv_g(b):
                load_g(GC + b, 0, conv_in_v[0, :, :, b * BLK:(b + 1) * BLK])

            def conv_u(b):
                load_u(UC + b, 0, conv_in_v[0, :, :, D + b * BLK:D + (b + 1) * BLK])

            def conv_d(b):
                load_d(DC + b, 0, conv_out_v[0, :, b * SUB:(b + 1) * SUB, :])

            def steady(f, b, i=0):
                ffn_g(f, b + 2, i)
                ffn_u(f, b + 2, i)
                ffn_d(f, b + 1, i)
                if b <= MOD_LAST[f]:
                    load_mod(MOD_AT[f] + b, i)

            def middle(f):
                steady(f, 0)
                with sp.Fori(0, LOOPS) as i:
                    steady(f, 1, i)
                    steady(f, 2, i)

            for dst, src in vec_loads[:VEC_LOADS // 2]:
                sp.dma_start(dst, src).then_inc(vec_in, 16)
            for v in range(4):
                load_mod(v, 0)
                if v == 1:
                    sp.dma_start(x_rows, x_v).then_inc(d_in[1], 16)
            for b in (0, 1):
                ffn_g(0, b)
                ffn_u(0, b)
            load_mod(MOD_PRE[0], 0)
            ffn_d(0, 0)
            middle(0)
            load_g(NB, 0, pool_v[0])
            ffn_u(1, 0)
            ffn_d(0, NB - 1)
            load_mod(MOD_AT[0] + NB - 2, 0)
            load_mod(MOD_AT[0] + NB - 1, 0)
            ffn_g(1, 0)
            ffn_u(1, 1)
            load_mod(MOD_PRE[1], 0)
            ffn_d(1, 0)
            ffn_g(1, 1)
            middle(1)
            ffn_g(2, 0)
            ffn_u(2, 0)
            ffn_d(1, NB - 1)
            ffn_g(2, 1)
            ffn_u(2, 1)
            ffn_d(2, 0)
            load_mod(MOD_PRE[2], 0)
            middle(2)
            conv_g(0)
            conv_u(0)
            ffn_d(2, NB - 1)
            conv_g(1)
            conv_u(1)
            conv_d(0)
            for b in range(2):
                conv_g(b + 2)
                conv_u(b + 2)
            conv_d(1)
            ffn_g(3, 0)
            ffn_u(3, 0)
            conv_d(2)
            ffn_g(3, 1)
            conv_d(3)
            ffn_u(3, 1)
            ffn_d(3, 0)
            middle(3)
            ffn_d(3, NB - 1)

            for n in range(PAIRS):
                sp.wait_ge(out_ready[n % 2], n // 2 + 1)
                cs = slice(n // 2 * (D // 2), (n // 2 + 1) * (D // 2))
                sp.dma_start(out_v[:, n % 2, cs], out_rows[:, n % 2, cs]).then_inc(stored, 16)
            sp.wait_ge(stored, 16 * PAIRS)

        @block.gpsimd
        def _(pool):
            nc.gpsimd.memset(ident[:], 0.0).then_inc(consts_step, 1)
            pool.wait_ge(consts_step, 1)
            nc.gpsimd.affine_select(out=ident[:], in_=ident[:], compare_op=ALU.not_equal, fill=1.0, base=0,
                                    pattern=[[-1, P]], channel_multiplier=1).then_inc(consts_ready, 1)
            nc.gpsimd.memset(mean_w[:], 1.0 / D).then_inc(consts_ready, 1)
            nc.gpsimd.memset(one[:], 1.0).then_inc(consts_ready, 1)
            nc.gpsimd.memset(eps[:], EPS).then_inc(consts_ready, 1)
            nc.gpsimd.memset(edge[:], 1.0).then_inc(consts_step, 1)
            pool.wait_ge(consts_step, 2)
            for g, w in enumerate(POOL_WINDOWS):
                nc.gpsimd.iota(edge[:, g, 0, 0:w // 2], pattern=[[1, w // 2]], base=w // 2, channel_multiplier=0,
                               allow_small_or_imprecise_dtypes=True).then_inc(consts_ready, 1)
                nc.gpsimd.iota(edge[:, g, 1, 0:w // 2], pattern=[[-1, w // 2]], base=w, channel_multiplier=0,
                               allow_small_or_imprecise_dtypes=True).then_inc(consts_ready, 1)
            nc.gpsimd.memset(wide[:], 0.0).then_inc(consts_ready, 1)

        @block.scalar
        def _(act):
            def hi_g(n, i=0):
                act.wait_ge(g_in[n % 2], 16 * (n // 2 + 2) + 16 * i)
                if n >= 2:
                    act.wait_ge(gu_done, n - 1 + 2 * i)
                nc.scalar.activation(g_hi[:, n % 2], g_raw[:, n % 2], ACT.Copy).then_inc(s_g_hi, 1)

            def hi_u(n, i=0):
                act.wait_ge(u_in[n % 2], 16 * (n // 2 + 2) + 16 * i)
                if n >= 2:
                    act.wait_ge(gu_done, (n - 1 if n - 2 < NB else n) + 2 * i)
                nc.scalar.activation(u_hi[:, n % 2], u_raw[:, n % 2], ACT.Copy).then_inc(s_u_hi, 1)

            def hi_d(n, i=0):
                act.wait_ge(d_in[n % 2], 16 * (n // 2 + 1 + n % 2) + 16 * i)
                if n >= 2:
                    act.wait_ge(d_done, n - 1 + 2 * i)
                nc.scalar.activation(d_hi[:, n % 2], d_raw[:, n % 2], ACT.Copy).then_inc(s_d_hi, 1)

            def block_out(f, b, i=0):
                e = NB * f + b
                act.wait_ge(gu_done, G0[f] + b + 1 + 2 * i)
                if e >= 1:
                    act.wait_ge(prod_ready, e + 2 * i)
                nc.scalar.activation(gated, ps_g[:], ACT.Silu).then_inc(gated_ready, 1)
                act.wait_ge(prod_ready, e + 1 + 2 * i)
                if b >= 2:
                    act.wait_ge(d_done, D0[f] + b - 1 + 2 * i)
                nc.scalar.activation(a_hi[:, b % 2].rearrange("p j t -> p (j t)"), prod, ACT.Copy).then_inc(a_hi_ready, 1)

            def steady(f, b, i=0):
                block_out(f, b, i)
                hi_g(G0[f] + b + 2, i)
                hi_u(U0[f] + b + 2, i)
                hi_d(D0[f] + b + 1, i)

            def middle(f):
                steady(f, 0)
                with act.Fori(0, LOOPS) as i:
                    steady(f, 1, i)
                    steady(f, 2, i)

            def norm_root(r, source, source_ready):
                nc.scalar.preload_act_table(ACT.Sqrt)
                for q in range(PAIRS):
                    act.wait_ge(*source_ready(q))
                    if q >= 2:
                        act.wait_ge(stat_step, PAIRS * r + q - 1)
                    nc.scalar.activation(sq[q % 2], source[:, 2 * q:2 * q + 2].rearrange("p k t -> p (k t)"),
                                         ACT.Square).then_inc(sq_ready, 1)
                act.wait_ge(stat_step, PAIRS * (r + 1))
                nc.scalar.activation(root, ps_stat[:, 0:L], ACT.Sqrt, bias=eps[:]).then_inc(root_ready, 1)
                nc.scalar.preload_act_table(ACT.Silu)

            def norm_tiles(r, shift):
                for k in range(KT):
                    act.wait_ge(scaled_ready, KT * r + k + 1)
                    ins = nc.scalar.activation(wide[:, k, PAD:PAD + L], scaled[k % 2], ACT.Identity,
                                               scale=coef[:, k:k + 1], bias=shift[:, k:k + 1])
                    if r == 1:
                        ins.then_inc(pool_in, 1)
                        continue
                    ins.then_inc(operand_ready, 1)
                    nc.scalar.activation(h_hi[:, k], scaled[k % 2], ACT.Identity,
                                         scale=coef[:, k:k + 1], bias=shift[:, k:k + 1]).then_inc(h_hi_ready, 1)

            def stage(s, layer, k):
                r = NORM_OF_STAGE[s]
                norm_root(r, xs, lambda q: (x_ready, PAIRS * s + q + 1))
                m = mod_at(layer, 3 * k)
                norm_tiles(r, mcol[:, m:m + KT])

            for dst, src in vec_loads[VEC_LOADS // 2:]:
                act.dma_start(dst, src).then_inc(vec_in, 16)
            nc.scalar.preload_act_table(ACT.Silu)
            act.wait_ge(cols_ready, 1)
            nc.scalar.activation(csilu[:], cols[:, C_COL:C_COL + KT], ACT.Silu).then_inc(csilu_ready, 1)
            act.wait_ge(consts_ready, CONSTS)
            norm_root(0, xs, lambda q: (x_ready, q + 1))
            hi_g(0)
            hi_u(0)
            norm_tiles(0, mcol[:, 0:KT])
            hi_g(1)
            hi_u(1)
            hi_d(0)

            middle(0)
            block_out(0, NB - 2)
            hi_g(NB)
            hi_u(NB)
            hi_d(NB - 1)
            block_out(0, NB - 1)
            hi_g(NB + 1)
            stage(1, 0, 1)
            for k in range(KT):
                act.wait_ge(operand_ready, KT + k + 1)
                nc.scalar.activation(h_hi[:, k], wide[:, k, PAD:PAD + L], ACT.Copy).then_inc(h_hi_ready, 1)
            hi_u(NB + 1)
            stage(2, 0, 2)
            hi_d(NB)
            hi_g(NB + 2)

            middle(1)
            for b in (NB - 2, NB - 1):
                steady(1, b)
            stage(3, 1, 0)

            middle(2)
            for b in (NB - 2, NB - 1):
                steady(2, b)
            stage(4, 1, 1)

            nc.scalar.preload_act_table(ACT.Sigmoid)
            act.wait_ge(h_lo_ready, KT * 5)
            for b in range(NC):
                act.wait_ge(gu_done, GC + b + 1)
                if b >= 1:
                    act.wait_ge(glu_ready, 2 * b)
                src = ps_u[:] if b % 2 == 0 else ps_d[:, 1]
                nc.scalar.activation(gated, src, ACT.Sigmoid).then_inc(glu_gate_ready, 1)
                if b < NC - 2:
                    hi_g(GC + b + 2)
                    hi_u(UC + b + 2)
                if b == NC - 2:
                    hi_d(DC + 1)
            nc.scalar.preload_act_table(ACT.Silu)
            n = 0
            for t in CONV_TILES_ON_PE:
                for w in range(TAPS):
                    if n >= DIAG_SLOTS:
                        act.wait_ge(diag_used, n - DIAG_SLOTS + 1)
                    col = DW + w * KT + t
                    nc.scalar.activation(diag[:, n % DIAG_SLOTS], ident[:], ACT.Copy,
                                         scale=cols[:, col:col + 1]).then_inc(diag_ready, 1)
                    n += 1
            hi_g(G0[3])
            hi_u(U0[3])
            norm_root(LN_NORM, conv, lambda q: (centred, q + 1))
            for k in range(KT):
                act.wait_ge(scaled_ready, KT * LN_NORM + k + 1)
                nc.scalar.activation(wide[:, k, PAD:PAD + L], scaled[k % 2], ACT.Silu, scale=cols[:, LN_G + k:LN_G + k + 1],
                                     bias=cols[:, LN_B + k:LN_B + k + 1]).then_inc(operand_ready, 1)
                act.wait_ge(operand_ready, KT * LN_NORM + k + 1)
                nc.scalar.activation(h_hi[:, k], wide[:, k, PAD:PAD + L], ACT.Copy).then_inc(h_hi_ready, 1)
            hi_d(DC + 2)
            hi_g(G0[3] + 1)
            hi_d(DC + 3)
            hi_u(U0[3] + 1)
            hi_d(D0[3])
            stage(5, 1, 2)

            middle(3)
            block_out(3, NB - 2)
            hi_d(D0[3] + NB - 1)
            block_out(3, NB - 1)
            r = NORM_OF_STAGE[6]
            norm_root(r, xs, lambda q: (x_ready, PAIRS * 6 + q + 1))
            for k in range(KT):
                act.wait_ge(scaled_ready, KT * r + k + 1)
                nc.scalar.activation(wide[:, k, PAD:PAD + L], scaled[k % 2], ACT.Copy,
                                     scale=cols[:, FINAL_G + k:FINAL_G + k + 1]).then_inc(operand_ready, 1)
            for n in (1, 3):
                act.wait_ge(out_psum, n + 1)
                nc.scalar.activation(out_rows[:, n % 2, n // 2 * 512:n // 2 * 512 + 512], ps_d[:, n], ACT.Copy).then_inc(out_ready[1], 1)

        @block.vector
        def _(dve):
            def lo_g(n, i=0):
                dve.wait_ge(s_g_hi, n + 1 + 2 * i)
                dve.tensor_tensor(g_lo[:, n % 2], g_raw[:, n % 2], f32(g_hi[:, n % 2]), ALU.subtract).then_inc(s_g_lo, 1)

            def lo_u(n, i=0):
                dve.wait_ge(s_u_hi, n + 1 + 2 * i)
                dve.tensor_tensor(u_lo[:, n % 2], u_raw[:, n % 2], f32(u_hi[:, n % 2]), ALU.subtract).then_inc(s_u_lo, 1)

            def lo_d(n, i=0):
                dve.wait_ge(s_d_hi, n + 1 + 2 * i)
                dve.tensor_tensor(d_lo[:, n % 2], d_raw[:, n % 2], f32(d_hi[:, n % 2]), ALU.subtract).then_inc(s_d_lo, 1)

            def mod_acc(v, i=0):
                raw = {1: g_raw, 2: u_raw}.get(v, m_raw)
                arrived = {1: g_in, 2: u_in}.get(v, m_in)
                if v >= 2:
                    dve.wait_ge(reduced, v - 1 + 2 * i)
                for k in range(KT):
                    if k % 4 == 0:
                        h = k // 4
                        w = raw[:, h].rearrange("p k n -> p (k n)")
                        dve.wait_ge(arrived[h], (16 * (v - 1) if v >= 3 else 16) + 32 * i)
                    wk = w[:, (k % 4) * MOD_COLS:(k % 4 + 1) * MOD_COLS]
                    if k == 0:
                        dve.tensor_scalar(acc[:, v % 2], wk, csilu[:, 0:1], None, ALU.mult).then_inc(acc_step, 1)
                    else:
                        dve.wait_ge(acc_step, 8 * v + k + 16 * i)
                        dve.scalar_tensor_tensor(out=acc[:, v % 2], in0=wk, scalar=csilu[:, k:k + 1], in1=acc[:, v % 2],
                                                 op0=ALU.mult, op1=ALU.add).then_inc(acc_step, 1)

            def mod_out(v, i=0):
                dve.wait_ge(reduced, v + 1 + 2 * i)
                dve.tensor_tensor(mcol[:, bass.ds(v * MOD_SUB + i * (2 * MOD_SUB), MOD_SUB)], ps_mod[:, 0:MOD_SUB],
                                  cols[:, bass.ds(MOD_B + v * MOD_SUB + i * (2 * MOD_SUB), MOD_SUB)],
                                  ALU.add).then_inc(mcol_ready, 1)

            def block_out(f, b, i=0):
                e = NB * f + b
                dve.wait_ge(gated_ready, e + 1 + 2 * i)
                if e >= 1:
                    dve.wait_ge(a_lo_ready, e + 2 * i)
                dve.tensor_tensor(prod, gated, ps_u[:], ALU.mult).then_inc(prod_ready, 1)
                dve.wait_ge(a_hi_ready, e + 1 + 2 * i)
                dve.tensor_tensor(a_lo[:, b % 2].rearrange("p j t -> p (j t)"), prod,
                                  f32(a_hi[:, b % 2].rearrange("p j t -> p (j t)")), ALU.subtract).then_inc(a_lo_ready, 1)

            def mods(f, b, i=0):
                if MOD_PRE[f] is not None and b - 1 <= MOD_LAST[f]:
                    mod_out(MOD_AT[f] + b - 1 if b else MOD_PRE[f], i)

            def steady(f, b, i=0):
                if b == 0 and f in (1, 2):
                    mod_acc(MOD_PRE[f])
                block_out(f, b, i)
                if b == 0 and f == 0:
                    mod_acc(MOD_PRE[f])
                lo_g(G0[f] + b + 2, i)
                lo_u(U0[f] + b + 2, i)
                lo_d(D0[f] + b + 1, i)
                mods(f, b, i)
                if b <= MOD_LAST[f]:
                    mod_acc(MOD_AT[f] + b, i)

            def middle(f):
                steady(f, 0)
                with dve.Fori(0, LOOPS) as i:
                    steady(f, 1, i)
                    steady(f, 2, i)

            def norm_coef(s, layer, k):
                g = NORM_G + (layer * 3 + k) * KT
                m = mod_at(layer, 3 * k + 1)
                dve.scalar_tensor_tensor(out=coef[:], in0=mcol[:, m:m + KT], scalar=1.0, in1=cols[:, g:g + KT],
                                         op0=ALU.add, op1=ALU.mult).then_inc(coef_ready, 1)

            def residual(s, wait, gate):
                for q in range(PAIRS):
                    dve.wait_ge(*wait(q))
                    for k in (2 * q, 2 * q + 1):
                        ins = dve.scalar_tensor_tensor(out=xs[:, k], in0=ps_d[:, q, (k % 2) * L:(k % 2 + 1) * L],
                                                       scalar=gate[:, k:k + 1], in1=xs[:, k], op0=ALU.mult, op1=ALU.add)
                    ins.then_inc(x_ready, 1)

            def norm_rstd(r):
                dve.wait_ge(root_ready, r + 1)
                dve.reciprocal(rstd, root).then_inc(rstd_ready, 1)
                dve.wait_ge(rstd_ready, r + 1)

            def scale_tile(r, k, source):
                if k >= 2:
                    if r == 1:
                        dve.wait_ge(pool_in, k - 1)
                    elif r == NORM_OF_STAGE[6]:
                        dve.wait_ge(operand_ready, KT * r + k - 1)
                    elif r == LN_NORM:
                        dve.wait_ge(operand_ready, KT * r + k - 1)
                    else:
                        dve.wait_ge(h_hi_ready, KT * r + k - 1)
                dve.tensor_tensor(scaled[k % 2], source[:, k], rstd, ALU.mult).then_inc(scaled_ready, 1)

            def norm_tiles(r):
                for k in range(KT):
                    scale_tile(r, k, xs)
                    if k >= 1 and r != 1:
                        norm_lo(r, k - 1)
                if r != 1:
                    norm_lo(r, KT - 1)

            def norm_lo(r, k):
                dve.wait_ge(h_hi_ready, KT * r + k + 1)
                dve.tensor_tensor(h_lo[:, k], wide[:, k, PAD:PAD + L], f32(h_hi[:, k]), ALU.subtract).then_inc(h_lo_ready, 1)

            def stage_norm(s):
                norm_rstd(NORM_OF_STAGE[s])
                norm_tiles(NORM_OF_STAGE[s])

            def half_gate(layer, k):
                m = mod_at(layer, 3 * k + 2)
                dve.tensor_scalar(gcoef[:], mcol[:, m:m + KT], 0.5, None, ALU.mult).then_inc(coef_ready, 1)

            def ffn_bank(f):
                k = [0, 2, 3, 5][f]
                return lambda q: (bank_ready, 3 * k + q + 1) if q < PAIRS - 1 else (d_done, D0[f] + NB)

            dve.wait_ge(cols_psum, 1)
            dve.tensor_copy(cols[:], ps_u[:, 0:N_COLS]).then_inc(cols_ready, 1)
            dve.wait_ge(csilu_ready, 1)
            mod_acc(0)
            mod_acc(1)
            mod_out(0)
            for q in range(PAIRS):
                dve.wait_ge(xt_ready, q + 1)
                dve.tensor_copy(xs[:, 2 * q:2 * q + 2].rearrange("p k t -> p (k t)"), ps_d[:, q]).then_inc(x_ready, 1)
            mod_acc(2)
            mod_out(1)
            norm_rstd(0)
            mod_acc(3)
            mod_out(2)
            mod_out(3)
            dve.wait_ge(mcol_ready, 4)
            norm_coef(0, 0, 0)
            lo_g(0)
            dve.wait_ge(coef_ready, 1)
            norm_tiles(0)
            lo_u(0)
            lo_g(1)
            lo_u(1)
            lo_d(0)

            middle(0)
            block_out(0, NB - 2)
            lo_g(NB)
            lo_u(NB)
            lo_d(NB - 1)
            mods(0, NB - 2)
            mod_acc(MOD_AT[0] + NB - 2)
            block_out(0, NB - 1)
            mod_acc(MOD_AT[0] + NB - 1)
            mods(0, NB - 1)
            dve.wait_ge(consts_ready, CONSTS)
            dve.reciprocal(edge[:], edge[:]).then_inc(edge_step, 1)
            dve.wait_ge(edge_step, 1)
            for g, w in enumerate(POOL_WINDOWS):
                dve.tensor_scalar(edge[:, g], edge[:, g], float(w), None, ALU.mult).then_inc(edge_step, 1)
            dve.wait_ge(mcol_ready, 15)
            norm_coef(1, 0, 1)
            half_gate(0, 0)
            dve.wait_ge(coef_ready, 3)
            residual(1, ffn_bank(0), gcoef)
            mod_out(MOD_AT[0] + NB - 1)
            stage_norm(1)
            dve.wait_ge(edge_step, 1 + len(POOL_WINDOWS))
            steps = 0
            for g, w in enumerate(POOL_WINDOWS):
                dve.wait_ge(pool_in, 2 * g + 2)
                if g >= 1:
                    dve.wait_ge(operand_ready, KT + 2 * g)
                ks = slice(2 * g, 2 * g + 2)
                first = PAD - w // 2
                n = L + w - 2
                cur = wide[:, ks, first:first + n + 1]
                half = 1
                turn = 0
                while half < w:
                    n = L + w - 2 * half
                    dst = run_sum[turn][:, :, 0:n]
                    dve.tensor_tensor(dst, cur[:, :, 0:n], cur[:, :, half:half + n], ALU.add).then_inc(pool_step, 1)
                    steps += 1
                    dve.wait_ge(pool_step, steps)
                    cur, half, turn = run_sum[turn], 2 * half, 1 - turn
                for e, at in enumerate((0, L - w // 2)):
                    piece = cur[:, :, at:at + w // 2]
                    dve.tensor_tensor(piece, piece, edge[:, g, e, 0:w // 2].unsqueeze(1).to_broadcast([P, 2, w // 2]),
                                      ALU.mult).then_inc(pool_step, 1)
                    steps += 1
                dve.wait_ge(pool_step, steps)
                for k in (0, 1):
                    own = wide[:, 2 * g + k, PAD:PAD + L]
                    dve.scalar_tensor_tensor(out=own, in0=cur[:, k, 0:L], scalar=1.0 / w, in1=own,
                                             op0=ALU.mult, op1=ALU.subtract).then_inc(operand_ready, 1)
                if g >= 1:
                    norm_lo(1, 2 * g - 2)
                    norm_lo(1, 2 * g - 1)
            norm_lo(1, KT - 2)
            norm_lo(1, KT - 1)
            m = mod_at(0, 5)
            dve.tensor_tensor(gcoef[:], mcol[:, m:m + KT], cols[:, POOL_SC:POOL_SC + KT], ALU.mult).then_inc(coef_ready, 1)
            dve.wait_ge(mcol_ready, 16)
            norm_coef(2, 0, 2)
            dve.wait_ge(coef_ready, 5)
            residual(2, lambda q: (bank_ready, 3 + q + 1) if q < PAIRS - 1 else (gu_done, NB + 1), gcoef)
            lo_g(NB + 1)
            lo_u(NB + 1)
            stage_norm(2)
            lo_d(NB)
            lo_g(NB + 2)

            middle(1)
            for b in (NB - 2, NB - 1):
                steady(1, b)
            dve.wait_ge(mcol_ready, 26)
            norm_coef(3, 1, 0)
            half_gate(0, 2)
            dve.wait_ge(coef_ready, 7)
            residual(3, ffn_bank(1), gcoef)
            stage_norm(3)

            middle(2)
            for b in (NB - 2, NB - 1):
                steady(2, b)
            dve.wait_ge(mcol_ready, 36)
            norm_coef(4, 1, 1)
            half_gate(1, 0)
            dve.wait_ge(coef_ready, 9)
            residual(4, ffn_bank(2), gcoef)
            stage_norm(4)

            def glu(b):
                dve.wait_ge(glu_gate_ready, b + 1)
                src = ps_g if b % 2 == 0 else ps_d[:, 0]
                for k in (0, 1):
                    dve.tensor_tensor(wide[:, 2 * b + k, PAD:PAD + L], gated[:, k * L:(k + 1) * L],
                                      src[:, k * L:(k + 1) * L], ALU.mult).then_inc(glu_ready, 1)

            taps_done = [0]

            def taps(tiles):
                dve.wait_ge(glu_ready, max(tiles) + 1)
                for w in range(TAPS):
                    for n, k in enumerate(tiles):
                        col = cols[:, DW + w * KT + k:DW + w * KT + k + 1]
                        src = wide[:, k, w:w + L]
                        if w == 0:
                            dve.tensor_scalar(conv[:, k], src, col, None, ALU.mult).then_inc(tap_step, 1)
                        else:
                            dve.wait_ge(tap_step, taps_done[0] - len(tiles) + 1)
                            dve.scalar_tensor_tensor(out=conv[:, k], in0=src, scalar=col, in1=conv[:, k],
                                                     op0=ALU.mult, op1=ALU.add).then_inc(tap_step, 1)
                        taps_done[0] += 1

            glu(0)
            lo_g(GC + 2)
            lo_u(UC + 2)
            taps((0,))
            glu(1)
            lo_g(GC + 3)
            lo_u(UC + 3)
            taps((1,))
            glu(2)
            lo_d(DC + 1)
            glu(3)
            taps((2, 3, 4))
            for k in CONV_TILES_ON_PE:
                dve.wait_ge(diag_used, TAPS * (CONV_TILES_ON_PE.index(k) + 1))
                dve.tensor_copy(conv[:, k], ps_d[:, CONV_BANK[k], 0:L]).then_inc(conv_ready, 1)
            dve.wait_ge(mu_ready, 1)
            for q in range(PAIRS):
                dve.tensor_tensor(conv[:, 2 * q:2 * q + 2], conv[:, 2 * q:2 * q + 2],
                                  ps_mod[:, 0:L].unsqueeze(1).to_broadcast([P, 2, L]), ALU.subtract).then_inc(centred, 1)
            norm_rstd(LN_NORM)
            for k in range(KT):
                scale_tile(LN_NORM, k, conv)
                if k >= 1:
                    norm_lo(LN_NORM, k - 1)
            norm_lo(LN_NORM, KT - 1)
            lo_g(G0[3])
            lo_u(U0[3])
            lo_d(DC + 2)
            lo_g(G0[3] + 1)
            lo_d(DC + 3)
            lo_u(U0[3] + 1)
            lo_d(D0[3])
            norm_coef(5, 1, 2)
            dve.wait_ge(coef_ready, 10)
            m = mod_at(1, 5)
            residual(5, lambda q: (bank_ready, 3 * 4 + q + 1) if q < PAIRS - 1 else (d_done, DC + NC), mcol[:, m:m + KT])
            stage_norm(5)

            middle(3)
            block_out(3, NB - 2)
            lo_d(D0[3] + NB - 1)
            block_out(3, NB - 1)
            half_gate(1, 2)
            dve.wait_ge(coef_ready, 11)
            residual(6, ffn_bank(3), gcoef)
            r = NORM_OF_STAGE[6]
            norm_rstd(r)
            scale_tile(r, 0, xs)
            for k in range(1, KT):
                scale_tile(r, k, xs)
            for n in (0, 2):
                dve.wait_ge(out_psum, n + 1)
                dve.tensor_copy(out_rows[:, n % 2, n // 2 * 512:n // 2 * 512 + 512], ps_d[:, n]).then_inc(out_ready[0], 1)

        @block.tensor
        def _(pe):
            def mm3(dst, w_hi, w_lo, m_hi, m_lo, start, stop):
                pe.matmul(dst, w_hi, m_hi, start=start, stop=False, skip_group_check=True)
                pe.matmul(dst, w_hi, m_lo, start=False, stop=False, skip_group_check=True)
                return pe.matmul(dst, w_lo, m_hi, start=False, stop=stop, skip_group_check=True)

            def gate_up(g, u, lo_from, i=0, banks=None):
                dst_g, dst_u = banks or (ps_g, ps_u)
                pe.wait_ge(s_g_lo, g + 1 + 2 * i)
                halves = [(dst_g, g_hi, g_lo, g % 2), (dst_u, u_hi, u_lo, u % 2)]
                if g > 0:
                    pe.wait_ge(s_u_lo, u + 1 + 2 * i)
                    order = [(k, halves) for k in range(KT)]
                else:
                    order = [(k, [half]) for half in halves for k in range(KT)]
                for n, (k, todo) in enumerate(order):
                    if lo_from is not None and n < KT:
                        pe.wait_ge(h_lo_ready, lo_from + k + 1)
                    if n == KT:
                        pe.wait_ge(s_u_lo, 1)
                    for dst, hi, lo, slot in todo:
                        for j in range(SUB):
                            mm = mm3(dst[:, j * L:(j + 1) * L], hi[:, slot, k, j * P:(j + 1) * P],
                                     lo[:, slot, k, j * P:(j + 1) * P], h_hi[:, k], h_lo[:, k],
                                     start=(k == 0 and j == 0), stop=(k == KT - 1))
                mm.then_inc(gu_done, 1)

            def ffn_block(f, b, i=0):
                e = NB * f + b
                if e >= 1:
                    pe.wait_ge(prod_ready, e + 2 * i)
                gate_up(G0[f] + b, U0[f] + b, KT * NORM_OF_STAGE[FFN_STAGE[f]] if b == 0 else None, i)

            def mod_reduce(v, i=0):
                pe.wait_ge(acc_step, 8 * (v + 1) + 16 * i)
                if v >= 1:
                    pe.wait_ge(mcol_ready, v + 2 * i)
                for j in range(MOD_SUB):
                    mm = pe.matmul(ps_mod[:, j:j + 1], acc[:, v % 2, j * P:(j + 1) * P], one[:], start=True, stop=True,
                                   skip_group_check=True)
                mm.then_inc(reduced, 1)

            def down_unit(d, first, m_hi, m_lo, tiles, i=0, stop=False):
                for j in range(SUB):
                    for k in tiles:
                        mm = mm3(ps_d[:, k // 2, (k % 2) * L:(k % 2 + 1) * L], d_hi[:, d % 2, j, k * P:(k + 1) * P],
                                 d_lo[:, d % 2, j, k * P:(k + 1) * P], m_hi(j), m_lo(j),
                                 start=(first and j == 0 and k % 2 == 0), stop=(stop and j == SUB - 1))
                return mm

            def last_down(d, m_hi, m_lo):
                for q in range(PAIRS):
                    mm = down_unit(d, False, m_hi, m_lo, (2 * q, 2 * q + 1), stop=True)
                    mm.then_inc(bank_ready if q < PAIRS - 1 else d_done, 1)

            def ffn_down(f, b, i=0):
                d = D0[f] + b
                pe.wait_ge(s_d_lo, d + 1 + 2 * i)
                pe.wait_ge(a_lo_ready, NB * f + b + 1 + 2 * i)
                m_hi, m_lo = (lambda j: a_hi[:, b % 2, j]), (lambda j: a_lo[:, b % 2, j])
                if b == NB - 1:
                    last_down(d, m_hi, m_lo)
                else:
                    down_unit(d, b == 0, m_hi, m_lo, range(KT), i).then_inc(d_done, 1)

            def steady(f, b, i=0):
                ffn_block(f, b, i)
                if f == 0 and b == 1:
                    mod_reduce(MOD_PRE[f])
                ffn_down(f, b - 1, i)
                if b - 1 <= MOD_LAST[f]:
                    mod_reduce(MOD_AT[f] + b - 1, i)

            def ffn(f):
                ffn_block(f, 0)
                if f in (1, 2):
                    mod_reduce(MOD_PRE[f])
                steady(f, 1)
                with pe.Fori(0, LOOPS) as i:
                    steady(f, 2, i)
                    steady(f, 3, i)
                steady(f, NB - 1)
                ffn_down(f, NB - 1)

            def stat(r):
                for q in range(PAIRS):
                    pe.wait_ge(sq_ready, PAIRS * r + q + 1)
                    for k in (0, 1):
                        mm = pe.matmul(ps_stat[:, 0:L], mean_w[:], sq[q % 2][:, k * L:(k + 1) * L],
                                       start=(q == 0 and k == 0), stop=(q == PAIRS - 1 and k == 1), skip_group_check=True)
                    mm.then_inc(stat_step, 1)

            pe.wait_ge(consts_ready, 3)
            pe.wait_ge(vec_in, 16 * VEC_LOADS)
            at = 0
            for r, n in enumerate((MOD_B, N_MOD * KT, N_MOD * KT, TAPS * KT // 2, TAPS * KT // 2)):
                mm = pe.transpose(ps_u[:, at:at + n], vec_rows[0:n, r, :], ident[0:n, 0:n])
                at += n
            mm.then_inc(cols_psum, 1)
            mod_reduce(0)
            pe.wait_ge(d_in[1], 16)
            for q in range(PAIRS):
                for k in (0, 1):
                    for a in range(L // P):
                        mm = pe.transpose(ps_d[:, q, k * L + a * P:k * L + (a + 1) * P],
                                          x_rows[:, a, (2 * q + k) * P:(2 * q + k + 1) * P], ident[:])
                mm.then_inc(xt_ready, 1)
            mod_reduce(1)
            stat(0)
            mod_reduce(2)
            mod_reduce(3)

            ffn(0)
            mod_reduce(MOD_AT[0] + NB - 1)
            stat(1)
            pe.wait_ge(s_g_lo, NB + 1)
            slot = NB % 2
            for g in range(len(POOL_WINDOWS)):
                pe.wait_ge(h_lo_ready, KT * 1 + 2 * g + 2)
                for m in range(SUB):
                    for j in range(SUB):
                        mm = mm3(ps_d[:, g, m * L:(m + 1) * L], g_hi[:, slot, 2 * g + j, m * P:(m + 1) * P],
                                 g_lo[:, slot, 2 * g + j, m * P:(m + 1) * P], h_hi[:, 2 * g + j], h_lo[:, 2 * g + j],
                                 start=(m == 0 and j == 0), stop=(j == SUB - 1))
                mm.then_inc(bank_ready if g < PAIRS - 1 else gu_done, 1)
            stat(2)

            for f in (1, 2):
                ffn(f)
                stat(NORM_OF_STAGE[f + 2])

            for b in range(NC):
                if b >= 2:
                    pe.wait_ge(glu_ready, 2 * (b - 1))
                gate_up(GC + b, UC + b, KT * 4 if b == 0 else None, banks=None if b % 2 == 0 else (ps_d[:, 0], ps_d[:, 1]))
            n = 0
            for t in CONV_TILES_ON_PE:
                pe.wait_ge(glu_ready, t + 1)
                for w in range(TAPS):
                    pe.wait_ge(diag_ready, n + 1)
                    mm = pe.matmul(ps_d[:, CONV_BANK[t], 0:L], diag[:, n % DIAG_SLOTS], wide[:, t, w:w + L],
                                   start=(w == 0), stop=(w == TAPS - 1), skip_group_check=True)
                    mm.then_inc(diag_used, 1)
                    n += 1
            pe.wait_ge(tap_step, TAPS * (KT - len(CONV_TILES_ON_PE)))
            pe.wait_ge(conv_ready, len(CONV_TILES_ON_PE))
            for k in range(KT):
                mm = pe.matmul(ps_mod[:, 0:L], mean_w[:], conv[:, k], start=(k == 0), stop=(k == KT - 1), skip_group_check=True)
            mm.then_inc(mu_ready, 1)
            stat(LN_NORM)
            for b in range(NC):
                pe.wait_ge(s_d_lo, DC + b + 1)
                if b == 0:
                    pe.wait_ge(h_lo_ready, KT * (LN_NORM + 1))
                m_hi, m_lo = (lambda j: h_hi[:, 2 * b + j]), (lambda j: h_lo[:, 2 * b + j])
                if b == NC - 1:
                    last_down(DC + b, m_hi, m_lo)
                else:
                    down_unit(DC + b, b == 0, m_hi, m_lo, range(KT)).then_inc(d_done, 1)
            stat(NORM_OF_STAGE[5])

            ffn(3)
            r = NORM_OF_STAGE[6]
            stat(r)
            for n in range(PAIRS):
                a, half = n % 2, n // 2
                for k in range(KT // 2):
                    dt = half * (KT // 2) + k
                    pe.wait_ge(operand_ready, KT * r + dt + 1)
                    mm = pe.transpose(ps_d[:, n, k * P:(k + 1) * P], wide[:, dt, PAD + a * P:PAD + (a + 1) * P], ident[:])
                mm.then_inc(out_psum, 1)


_INS = ['x', 'c', 'mod_w', 'mod_b', 'norm_g', 'final_g', 'ffn_w_gate', 'ffn_w_up', 'ffn_w_down', 'pool_w',
        'pool_scale', 'conv_w_in', 'conv_dw', 'conv_ln_g', 'conv_ln_b', 'conv_w_out']


def kernel(**inputs):
    import numpy as _np
    import concourse.bacc as _bacc
    from concourse import mybir as _mybir
    from concourse.bass_utils import run_bass_kernel_spmd as _run

    nc = _bacc.Bacc("TRN2", target_bir_lowering=False, num_devices=1,
                    dynamic_dma_scratch_size=1024)
    arrays, args = {}, []
    for name in _INS:
        a = _np.ascontiguousarray(inputs[name])
        arrays[f"in_{name}_dram"] = a
        args.append(nc.dram_tensor(f"in_{name}_dram", a.shape, _mybir.dt.from_np(a.dtype), kind="ExternalInput").ap())
    x = inputs['x']
    out = nc.dram_tensor("out_0_dram", x.shape, _mybir.dt.from_np(_np.dtype(x.dtype)), kind="ExternalOutput").ap()
    backbone_kernel(nc, *args, out)
    r = _run(nc, [arrays], core_ids=[0])
    return r.results[0]["out_0_dram"]
```

```python
from contextlib import ExitStack

import concourse.bass as bass
from concourse import mybir

ALU = mybir.AluOpType
AX = mybir.AxisListType
ACT = mybir.ActivationFunctionType
F32 = mybir.dt.float32
F32R = mybir.dt.float32r

P = 128
EPS = 1e-6
POOL_WINDOWS = (2, 4, 8, 16)
PAD = 15
MOD_COLS = 512
BLK = 256
SUB = BLK // P
WARM = 20
PRE_STEPS = 6
DIAG_SLOTS = 8
SQ = 32
CONV_TILES_ON_PE = (5, 6, 7)


def backbone_kernel(nc, x, c, mod_w, mod_b, norm_g, final_g, ffn_w_gate, ffn_w_up, ffn_w_down,
                    pool_w, pool_scale, conv_w_in, conv_dw, conv_ln_g, conv_ln_b, conv_w_out, out):
    _, L, D = x.shape
    DEPTH, _, _, FF = ffn_w_gate.shape
    TAPS = conv_dw.shape[1]
    KT = D // P
    NB = FF // BLK
    NC = D // BLK
    PAIRS = KT // 2
    N_MOD = mod_w.shape[2] // D
    MOD_UNITS = N_MOD * D // MOD_COLS
    MOD_SUB = MOD_COLS // P
    WIDTH = L + 2 * PAD
    REACH = P + max(POOL_WINDOWS) // 2
    LOOPS = (NB - 3) // 2
    assert DEPTH == 2 and L == 256 and KT == 8 and NB == 11 and NC == 4 and TAPS == 2 * PAD + 1
    assert MOD_UNITS == 18

    G0 = [0, NB + 1, 2 * NB + 1, 3 * NB + 1 + NC]
    U0 = [0, NB, 2 * NB, 3 * NB + NC]
    D0 = [0, NB, 2 * NB, 3 * NB + NC]
    GC, UC, DC = 3 * NB + 1, 3 * NB, 3 * NB
    MOD_AT = [4, 16, 26, None]
    MOD_LAST = [NB - 3, NB - 2, NB - 2, -1]
    MOD_MORE = MOD_AT[0] + NB - 2
    MOD_GROUPS = [(0, 4), (4, 14), (14, 16), (16, 26), (26, 36)]
    D_LAST = D0[3] + NB - 2

    NORM_G, FINAL_G = 0, DEPTH * 3 * KT
    POOL_SC, LN_G, LN_B, MOD_B = (FINAL_G + (j + 1) * KT for j in range(4))
    DW = MOD_B + DEPTH * N_MOD * KT
    N_COLS = DW + TAPS * KT

    with ExitStack() as ctx:
        def sb(name, shape, dt=F32):
            return ctx.enter_context(nc.sbuf_tensor(name, shape, dt))

        def psum(name, shape):
            return ctx.enter_context(nc.psum_tensor(name, shape, F32))

        def sem(name):
            return ctx.enter_context(nc.semaphore(name))

        g_raw, u_raw = sb("g_raw", [P, 2, KT, BLK]), sb("u_raw", [P, 2, KT, BLK])
        d_raw = sb("d_raw", [P, 2, SUB, D])
        g_hi, g_lo = sb("g_hi", [P, 2, KT, BLK], F32R), sb("g_lo", [P, 2, KT, BLK], F32R)
        u_hi, u_lo = sb("u_hi", [P, 2, KT, BLK], F32R), sb("u_lo", [P, 2, KT, BLK], F32R)
        d_hi, d_lo = sb("d_hi", [P, 2, SUB, D], F32R), sb("d_lo", [P, 2, SUB, D], F32R)
        m_raw = sb("m_raw", [P, 2, KT // 2, MOD_COLS])
        xs = sb("xs", [P, KT, L])
        wide = sb("wide", [P, KT, WIDTH])
        h_hi, h_lo = sb("h_hi", [P, KT, L], F32R), sb("h_lo", [P, KT, L], F32R)
        a_hi, a_lo = sb("a_hi", [P, 2, SUB, L], F32R), sb("a_lo", [P, 2, SUB, L], F32R)
        scr = sb("scr", [P, 2048])
        cols = sb("cols", [P, N_COLS])
        mcol = sb("mcol", [P, DEPTH * N_MOD * KT])
        acc = sb("acc", [P, MOD_COLS])
        turned = sb("turned", [P, MOD_COLS])
        part = sb("part", [P, DEPTH * MOD_UNITS, MOD_COLS // SQ])
        csilu = sb("csilu", [P, KT])
        coef = sb("coef", [P, KT])
        gcoef = sb("gcoef", [P, KT])
        edge = sb("edge", [P, len(POOL_WINDOWS), 2, max(POOL_WINDOWS) // 2])
        eps = sb("eps", [P, 1])
        pool_mat = sb("pool_mat", [P, len(POOL_WINDOWS), L // P, REACH])
        mean_w = sb("mean_w", [P, P])
        ident = sb("ident", [P, P])

        x_rows = d_raw[:, 1]
        out_rows = d_raw[:, D_LAST % 2]
        conv = m_raw[:].rearrange("p a k n -> p (a k n)")[:, 0:KT * L].rearrange("p (k t) -> p k t", k=KT)
        vec_rows = scr[:, 1280:1280 + 5 * P].rearrange("p (r n) -> p r n", r=5)
        c_rows = scr[0:KT, 2048 - P:2048]
        gated = scr[:, 0:512]
        prod = scr[:, 512:1024]
        sq = [scr[:, 512 * j:512 * (j + 1)] for j in range(2)]
        gather = scr[:, 1024:1024 + 2 * P - SQ]
        rstd = scr[:, 1280:1536]
        scaled = [scr[:, 1536 + 256 * j:1792 + 256 * j] for j in range(2)]
        pool_rows = [scr[:, 512 * j:512 * (j + 1)] for j in range(2)]
        diag = scr[:, 1024:1024 + DIAG_SLOTS * P].rearrange("p (s n) -> p s n", s=DIAG_SLOTS)

        ps_g, ps_u, ps_mod, ps_stat = (psum(n, [P, 512]) for n in ("ps_g", "ps_u", "ps_mod", "ps_stat"))
        ps_d = psum("ps_d", [P, PAIRS, 512])
        first_g, first_u = ps_d[:, 2], ps_d[:, 3]
        CONV_BANK = dict(zip(CONV_TILES_ON_PE, (3, 2, 0)))

        c_in, vec_in, stored = sem("c_in"), sem("vec_in"), sem("stored")
        g_in, u_in = [sem("g_in0"), sem("g_in1")], [sem("u_in0"), sem("u_in1")]
        m_in, d_in = [sem("m_in0"), sem("m_in1")], [sem("d_in0"), sem("d_in1")]
        s_g_hi, s_g_lo, s_u_hi, s_u_lo = sem("g_hi_ready"), sem("g_lo_ready"), sem("u_hi_ready"), sem("u_lo_ready")
        s_d_hi, s_d_lo = sem("d_hi_ready"), sem("d_lo_ready")
        gu_done, d_done = sem("gu_done"), sem("d_done")
        acc_step, turned_ready, part_ready = sem("acc_step"), sem("turned_ready"), sem("part_ready")
        reduced, mcol_ready = sem("reduced"), sem("mcol_ready")
        gated_ready, prod_ready, a_hi_ready, a_lo_ready = (
            sem("gated_ready"), sem("prod_ready"), sem("a_hi_ready"), sem("a_lo_ready"))
        bank_ready, x_ready, sq_ready, stat_step = sem("bank_ready"), sem("x_ready"), sem("sq_ready"), sem("stat_step")
        root_ready, rstd_ready, coef_ready = sem("root_ready"), sem("rstd_ready"), sem("coef_ready")
        scaled_ready, operand_ready, h_hi_ready, h_lo_ready = (
            sem("scaled_ready"), sem("operand_ready"), sem("h_hi_ready"), sem("h_lo_ready"))
        consts_ready, consts_step, c_psum, xt_ready, cols_psum, cols_ready, csilu_ready = (
            sem("consts_ready"), sem("consts_step"), sem("c_psum"), sem("xt_ready"), sem("cols_psum"),
            sem("cols_ready"), sem("csilu_ready"))
        edge_ready, share_ready, rows_psum, rows_ready = (
            sem("edge_ready"), sem("share_ready"), sem("rows_psum"), sem("rows_ready"))
        glu_gate_ready, glu_ready, tap_step, diag_ready, diag_used, conv_ready = (
            sem("glu_gate_ready"), sem("glu_ready"), sem("tap_step"), sem("diag_ready"), sem("diag_used"),
            sem("conv_ready"))
        mu_ready, centred = sem("mu_ready"), sem("centred")
        out_psum, out_ready = sem("out_psum"), [sem("out_ready_dve"), sem("out_ready_act")]

        gate_v = ffn_w_gate.rearrange("l f (k p) n -> l f p k n", p=P)
        up_v = ffn_w_up.rearrange("l f (k p) n -> l f p k n", p=P)
        down_v = ffn_w_down.rearrange("l f (j p) n -> l f p j n", p=P)
        mod_v = mod_w.rearrange("l (k p) n -> l p k n", p=P)
        conv_in_v = conv_w_in.rearrange("l (k p) n -> l p k n", p=P)
        conv_out_v = conv_w_out.rearrange("l (j p) n -> l p j n", p=P)
        pool_v = pool_w.rearrange("l g (j p) n -> l p (g j) n", p=P)
        x_v = x.rearrange("b (a p) d -> (b p) a d", p=P)
        out_v = out.rearrange("b (a p) d -> (b p) a d", p=P)

        NORM_OF_STAGE = [0, 1, 2, 3, 4, 6, 7]
        LN_NORM = 5
        FFN_STAGE = [0, 2, 3, 5]
        FFN_LAYER = [0, 0, 1, 1]

        CONSTS = 4
        POOL_CONSTS = CONSTS + len(POOL_WINDOWS) * (L // P)

        half_dw = TAPS * KT // 2
        dw_rows = conv_dw.rearrange("l w (k n) -> (l w k) n", n=P)
        vec_loads = [
            (vec_rows[NORM_G:FINAL_G, 0], norm_g.rearrange("l r (k n) -> (l r k) n", n=P)),
            (vec_rows[FINAL_G:POOL_SC, 0], final_g.rearrange("(k n) -> k n", n=P)),
            (vec_rows[POOL_SC:LN_G, 0], pool_scale.rearrange("l (k n) -> (l k) n", n=P)),
            (vec_rows[LN_G:LN_B, 0], conv_ln_g.rearrange("l (k n) -> (l k) n", n=P)),
            (vec_rows[LN_B:MOD_B, 0], conv_ln_b.rearrange("l (k n) -> (l k) n", n=P)),
        ]
        vec_loads.append((vec_rows[0:N_MOD * KT, 1:3], mod_b.rearrange("l (k n) -> k l n", n=P)))
        vec_loads.append((vec_rows[0:half_dw, 3:5], dw_rows.rearrange("(j r) n -> r j n", j=2)))
        VEC_LOADS = len(vec_loads)

        def mod_at(layer, k):
            return (layer * N_MOD + k) * KT

        def unit_at(v):
            for first, last in ((MOD_AT[0], MOD_MORE), (MOD_AT[1], MOD_AT[1] + NB - 2)):
                if first <= v <= last:
                    return first if v == last else v + 1
            return v

        def f32(ap):
            return ap.bitcast(F32)

        block = ctx.enter_context(nc.Block())

        @block.sync
        def _(sp):
            def load_g(n, i, src):
                if n >= 2:
                    sp.wait_ge(s_g_lo, n - 1 + 2 * i)
                else:
                    sp.wait_ge(acc_step, 4 * (3 + n))
                sp.dma_start(g_raw[:, n % 2], src).then_inc(g_in[n % 2], 16)

            def load_u(n, i, src):
                if n >= 2:
                    sp.wait_ge(s_u_lo, n - 1 + 2 * i)
                else:
                    sp.wait_ge(acc_step, 4 * (5 + n))
                sp.dma_start(u_raw[:, n % 2], src).then_inc(u_in[n % 2], 16)

            def load_d(n, i, src):
                if n >= 2:
                    sp.wait_ge(s_d_lo, n - 1 + 2 * i)
                elif n == 1:
                    sp.wait_ge(xt_ready, PAIRS)
                sp.dma_start(d_raw[:, n % 2], src).then_inc(d_in[n % 2], 16)

            def load_mod(v, i):
                u = unit_at(v)
                layer = u // MOD_UNITS
                for h in range(2):
                    src = mod_v[layer, :, 4 * h:4 * h + 4, bass.ds((u - layer * MOD_UNITS) * MOD_COLS + i * (2 * MOD_COLS), MOD_COLS)]
                    if v == 1:
                        sp.dma_start(g_raw[:, h].rearrange("p k n -> p (k n)").rearrange("p (k n) -> p k n", n=MOD_COLS), src).then_inc(g_in[h], 16)
                    elif v == 2:
                        sp.dma_start(u_raw[:, h].rearrange("p k n -> p (k n)").rearrange("p (k n) -> p k n", n=MOD_COLS), src).then_inc(u_in[h], 16)
                    else:
                        if v == 3:
                            sp.wait_ge(acc_step, 4 * (h + 1))
                        elif v >= 4:
                            sp.wait_ge(acc_step, 8 * v + 4 * h - 4 + 16 * i)
                        sp.dma_start(m_raw[:, h], src).then_inc(m_in[h], 16)

            def ffn_g(f, b, i=0):
                load_g(G0[f] + b, i, gate_v[FFN_LAYER[f], f % 2, :, :, bass.ds(b * BLK + i * (2 * BLK), BLK)])

            def ffn_u(f, b, i=0):
                load_u(U0[f] + b, i, up_v[FFN_LAYER[f], f % 2, :, :, bass.ds(b * BLK + i * (2 * BLK), BLK)])

            def ffn_d(f, b, i=0):
                load_d(D0[f] + b, i, down_v[FFN_LAYER[f], f % 2, :, bass.ds(b * SUB + i * (2 * SUB), SUB), :])

            def conv_g(b):
                load_g(GC + b, 0, conv_in_v[0, :, :, b * BLK:(b + 1) * BLK])

            def conv_u(b):
                load_u(UC + b, 0, conv_in_v[0, :, :, D + b * BLK:D + (b + 1) * BLK])

            def conv_d(b):
                load_d(DC + b, 0, conv_out_v[0, :, b * SUB:(b + 1) * SUB, :])

            def steady(f, b, i=0):
                ffn_g(f, b + 2, i)
                ffn_u(f, b + 2, i)
                ffn_d(f, b + 1, i)
                if b <= MOD_LAST[f]:
                    load_mod(MOD_AT[f] + b, i)

            def middle(f):
                steady(f, 0)
                with sp.Fori(0, LOOPS) as i:
                    steady(f, 1, i)
                    steady(f, 2, i)

            sp.dma_start(c_rows, c.rearrange("b (k n) -> (b k) n", n=P)).then_inc(c_in, 16)
            for v in range(4):
                load_mod(v, 0)
                if v == 1:
                    sp.dma_start(x_rows, x_v).then_inc(d_in[1], 16)
            for b in (0, 1):
                ffn_g(0, b)
                ffn_u(0, b)
            ffn_d(0, 0)
            middle(0)
            load_g(NB, 0, pool_v[0])
            ffn_u(1, 0)
            ffn_d(0, NB - 1)
            load_mod(MOD_MORE, 0)
            ffn_g(1, 0)
            ffn_u(1, 1)
            load_mod(MOD_MORE + 1, 0)
            ffn_d(1, 0)
            ffn_g(1, 1)
            load_mod(MOD_MORE + 2, 0)
            middle(1)
            ffn_g(2, 0)
            ffn_u(2, 0)
            ffn_d(1, NB - 1)
            load_mod(MOD_AT[1] + NB - 2, 0)
            ffn_g(2, 1)
            ffn_u(2, 1)
            ffn_d(2, 0)
            middle(2)
            conv_g(0)
            conv_u(0)
            ffn_d(2, NB - 1)
            load_mod(MOD_AT[2] + NB - 2, 0)
            conv_g(1)
            conv_u(1)
            conv_d(0)
            for b in range(2):
                conv_g(b + 2)
                conv_u(b + 2)
            conv_d(1)
            ffn_g(3, 0)
            ffn_u(3, 0)
            conv_d(2)
            ffn_g(3, 1)
            conv_d(3)
            ffn_u(3, 1)
            ffn_d(3, 0)
            middle(3)
            ffn_d(3, NB - 1)

            for n in range(PAIRS):
                sp.wait_ge(out_ready[n % 2], n // 2 + 1)
                cs = slice(n // 2 * (D // 2), (n // 2 + 1) * (D // 2))
                sp.dma_start(out_v[:, n % 2, cs], out_rows[:, n % 2, cs]).then_inc(stored, 16)
            sp.wait_ge(stored, 16 * PAIRS)

        @block.gpsimd
        def _(pool):
            nc.gpsimd.memset(ident[:], 0.0).then_inc(consts_step, 1)
            pool.wait_ge(consts_step, 1)
            nc.gpsimd.affine_select(out=ident[:], in_=ident[:], compare_op=ALU.not_equal, fill=1.0, base=0,
                                    pattern=[[-1, P]], channel_multiplier=1).then_inc(consts_ready, 1)
            nc.gpsimd.memset(mean_w[:], 1.0 / D).then_inc(consts_ready, 1)
            nc.gpsimd.memset(gather, 0.0).then_inc(consts_step, 1)
            for b in range(P // SQ):
                pool.wait_ge(consts_step, 2 + b)
                nc.gpsimd.affine_select(out=gather[:, P - SQ:P], in_=gather[:, P - SQ:P], compare_op=ALU.not_equal,
                                        fill=1.0, base=-SQ * b, pattern=[[-1, SQ]],
                                        channel_multiplier=1).then_inc(consts_step, 1)
            nc.gpsimd.memset(eps[:], EPS).then_inc(consts_ready, 1)
            nc.gpsimd.memset(wide[:], 0.0).then_inc(consts_ready, 1)
            nc.gpsimd.memset(edge[:], 1.0).then_inc(consts_step, 1)
            pool.wait_ge(consts_step, 3 + P // SQ)
            for g, w in enumerate(POOL_WINDOWS):
                nc.gpsimd.iota(edge[:, g, 0, 0:w // 2], pattern=[[1, w // 2]], base=w // 2, channel_multiplier=0,
                               allow_small_or_imprecise_dtypes=True).then_inc(edge_ready, 1)
                nc.gpsimd.iota(edge[:, g, 1, 0:w // 2], pattern=[[-1, w // 2]], base=w, channel_multiplier=0,
                               allow_small_or_imprecise_dtypes=True).then_inc(edge_ready, 1)
            pool.wait_ge(share_ready, 1)
            step = 3 + P // SQ
            for g, w in enumerate(POOL_WINDOWS):
                mat = pool_mat[:, g]
                nc.gpsimd.memset(mat, 1.0 / w).then_inc(consts_step, 1)
                step += 1
                pool.wait_ge(consts_step, step)
                for a, at in enumerate((0, REACH - w // 2)):
                    nc.gpsimd.tensor_copy(mat[:, a, at:at + w // 2], edge[:, g, a, 0:w // 2]).then_inc(consts_step, 1)
                    step += 1
                pool.wait_ge(consts_step, step)
                for a in range(L // P):
                    nc.gpsimd.affine_select(out=mat[:, a], in_=mat[:, a], compare_op=ALU.is_ge, fill=0.0,
                                            base=(P + REACH - L) * a + w // 2, pattern=[[-1, REACH]], channel_multiplier=1).then_inc(consts_step, 1)
                step += L // P
                pool.wait_ge(consts_step, step)
                for a in range(L // P):
                    nc.gpsimd.affine_select(out=mat[:, a], in_=mat[:, a], compare_op=ALU.is_ge, fill=0.0,
                                            base=w // 2 - 1 - (P + REACH - L) * a, pattern=[[1, REACH]], channel_multiplier=-1).then_inc(consts_step, 1)
                step += L // P
                pool.wait_ge(consts_step, step)
                for a in range(L // P):
                    own = mat[:, a, (P + REACH - L) * a:(P + REACH - L) * a + P]
                    nc.gpsimd.tensor_tensor(own, own, ident[:], ALU.subtract).then_inc(consts_ready, 1)

        @block.scalar
        def _(act):
            def hi_g(n, i=0):
                act.wait_ge(g_in[n % 2], 16 * (n // 2 + 2) + 16 * i)
                if n >= 2:
                    act.wait_ge(gu_done, n - 1 + 2 * i)
                nc.scalar.activation(g_hi[:, n % 2], g_raw[:, n % 2], ACT.Copy).then_inc(s_g_hi, 1)

            def hi_u(n, i=0):
                act.wait_ge(u_in[n % 2], 16 * (n // 2 + 2) + 16 * i)
                if n >= 2:
                    act.wait_ge(gu_done, (n - 1 if n - 2 < NB else n) + 2 * i)
                nc.scalar.activation(u_hi[:, n % 2], u_raw[:, n % 2], ACT.Copy).then_inc(s_u_hi, 1)

            def hi_d(n, i=0):
                act.wait_ge(d_in[n % 2], 16 * (n // 2 + 1 + n % 2) + 16 * i)
                if n >= 2:
                    act.wait_ge(d_done, n - 1 + 2 * i)
                nc.scalar.activation(d_hi[:, n % 2], d_raw[:, n % 2], ACT.Copy).then_inc(s_d_hi, 1)

            def block_gate(f, b, i=0):
                e = NB * f + b
                act.wait_ge(gu_done, G0[f] + b + 1 + 2 * i)
                if e >= 1:
                    act.wait_ge(prod_ready, e + 2 * i)
                nc.scalar.activation(gated, (ps_g if b else first_g)[:], ACT.Silu).then_inc(gated_ready, 1)

            def block_hi(f, b, i=0):
                act.wait_ge(prod_ready, NB * f + b + 1 + 2 * i)
                if b >= 2:
                    act.wait_ge(d_done, D0[f] + b - 1 + 2 * i)
                nc.scalar.activation(a_hi[:, b % 2].rearrange("p j t -> p (j t)"), prod, ACT.Copy).then_inc(a_hi_ready, 1)

            def steady(f, b, i=0):
                block_gate(f, b, i)
                hi_g(G0[f] + b + 2, i)
                block_hi(f, b, i)
                hi_u(U0[f] + b + 2, i)
                hi_d(D0[f] + b + 1, i)

            def middle(f):
                steady(f, 0)
                with act.Fori(0, LOOPS) as i:
                    steady(f, 1, i)
                    steady(f, 2, i)

            def norm_root(r, source, source_ready, squares_free=None):
                nc.scalar.preload_act_table(ACT.Sqrt)
                if squares_free:
                    act.wait_ge(*squares_free)
                for q in range(PAIRS):
                    act.wait_ge(*source_ready(q))
                    if q >= 2:
                        act.wait_ge(stat_step, PAIRS * r + q - 1)
                    nc.scalar.activation(sq[q % 2], source[:, 2 * q:2 * q + 2].rearrange("p k t -> p (k t)"),
                                         ACT.Square).then_inc(sq_ready, 1)
                act.wait_ge(stat_step, PAIRS * (r + 1))
                nc.scalar.activation(rstd, ps_stat[:, 0:L], ACT.Sqrt, bias=eps[:]).then_inc(root_ready, 1)
                nc.scalar.preload_act_table(ACT.Silu)

            def norm_tiles(r, shift):
                for k in range(KT):
                    act.wait_ge(scaled_ready, KT * r + k + 1)
                    nc.scalar.activation(wide[:, k, PAD:PAD + L], scaled[k % 2], ACT.Identity,
                                         scale=coef[:, k:k + 1], bias=shift[:, k:k + 1]).then_inc(operand_ready, 1)
                    nc.scalar.activation(h_hi[:, k], scaled[k % 2], ACT.Identity,
                                         scale=coef[:, k:k + 1], bias=shift[:, k:k + 1]).then_inc(h_hi_ready, 1)

            def stage(s, layer, k):
                r = NORM_OF_STAGE[s]
                norm_root(r, xs, lambda q: (x_ready, PAIRS * s + q + 1))
                m = mod_at(layer, 3 * k)
                norm_tiles(r, mcol[:, m:m + KT])

            nc.scalar.preload_act_table(ACT.Silu)
            for dst, src in vec_loads:
                act.dma_start(dst, src).then_inc(vec_in, 16)
            act.wait_ge(c_psum, 1)
            nc.scalar.activation(csilu[:], ps_mod[:, 0:KT], ACT.Silu).then_inc(csilu_ready, 1)
            for q in range(PAIRS):
                act.wait_ge(xt_ready, q + 1)
                nc.scalar.activation(xs[:, 2 * q:2 * q + 2].rearrange("p k t -> p (k t)"), ps_d[:, q], ACT.Copy).then_inc(x_ready, 1)
            act.wait_ge(consts_ready, CONSTS)
            norm_root(0, xs, lambda q: (x_ready, q + 1))
            hi_g(0)
            hi_u(0)
            norm_tiles(0, mcol[:, 0:KT])
            hi_g(1)
            hi_u(1)
            hi_d(0)

            middle(0)
            steady(0, NB - 2)
            block_gate(0, NB - 1)
            block_hi(0, NB - 1)
            hi_g(NB + 1)
            stage(1, 0, 1)
            hi_u(NB + 1)
            hi_d(NB)
            norm_root(2, xs, lambda q: (x_ready, PAIRS * 2 + q + 1), (gu_done, NB + 1))
            hi_g(NB + 2)
            norm_tiles(2, mcol[:, mod_at(0, 6):mod_at(0, 6) + KT])

            middle(1)
            for b in (NB - 2, NB - 1):
                steady(1, b)
            stage(3, 1, 0)

            middle(2)
            for b in (NB - 2, NB - 1):
                steady(2, b)
            stage(4, 1, 1)

            nc.scalar.preload_act_table(ACT.Sigmoid)
            act.wait_ge(h_lo_ready, KT * 5)
            n = [0]

            def diag_tap(upto):
                while n[0] < upto:
                    if n[0] >= DIAG_SLOTS:
                        act.wait_ge(diag_used, n[0] - DIAG_SLOTS + 1)
                    col = DW + n[0] % TAPS * KT + CONV_TILES_ON_PE[n[0] // TAPS]
                    nc.scalar.activation(diag[:, n[0] % DIAG_SLOTS], ident[:], ACT.Copy,
                                         scale=cols[:, col:col + 1]).then_inc(diag_ready, 1)
                    n[0] += 1

            for b in range(NC):
                act.wait_ge(gu_done, GC + b + 1)
                if b >= 1:
                    act.wait_ge(glu_ready, 2 * b)
                src = ps_u[:] if b % 2 == 0 else ps_d[:, 1]
                nc.scalar.activation(gated, src, ACT.Sigmoid).then_inc(glu_gate_ready, 1)
                if b < NC - 2:
                    hi_g(GC + b + 2)
                    hi_u(UC + b + 2)
                if b == NC - 2:
                    hi_d(DC + 1)
                    diag_tap(DIAG_SLOTS)
            nc.scalar.preload_act_table(ACT.Silu)
            for j, t in enumerate(CONV_TILES_ON_PE):
                diag_tap(min(TAPS * (j + 1) + DIAG_SLOTS, TAPS * len(CONV_TILES_ON_PE)))
                act.wait_ge(diag_used, TAPS * (j + 1))
                nc.scalar.activation(conv[:, t], ps_d[:, CONV_BANK[t], 0:L], ACT.Copy).then_inc(conv_ready, 1)
            hi_g(G0[3])
            hi_u(U0[3])
            norm_root(LN_NORM, conv, lambda q: (centred, q + 1))
            for k in range(KT):
                act.wait_ge(scaled_ready, KT * LN_NORM + k + 1)
                nc.scalar.activation(wide[:, k, PAD:PAD + L], scaled[k % 2], ACT.Silu, scale=cols[:, LN_G + k:LN_G + k + 1],
                                     bias=cols[:, LN_B + k:LN_B + k + 1]).then_inc(operand_ready, 1)
                act.wait_ge(operand_ready, KT * LN_NORM + k + 1)
                nc.scalar.activation(h_hi[:, k], wide[:, k, PAD:PAD + L], ACT.Copy).then_inc(h_hi_ready, 1)
            hi_d(DC + 2)
            hi_g(G0[3] + 1)
            hi_d(DC + 3)
            hi_u(U0[3] + 1)
            hi_d(D0[3])
            stage(5, 1, 2)

            middle(3)
            block_gate(3, NB - 2)
            block_hi(3, NB - 2)
            hi_d(D0[3] + NB - 1)
            block_gate(3, NB - 1)
            block_hi(3, NB - 1)
            r = NORM_OF_STAGE[6]
            norm_root(r, xs, lambda q: (x_ready, PAIRS * 6 + q + 1))
            for k in range(KT):
                act.wait_ge(scaled_ready, KT * r + k + 1)
                nc.scalar.activation(wide[:, k, PAD:PAD + L], scaled[k % 2], ACT.Copy,
                                     scale=cols[:, FINAL_G + k:FINAL_G + k + 1]).then_inc(operand_ready, 1)
            for n in (1, 3):
                act.wait_ge(out_psum, n + 1)
                nc.scalar.activation(out_rows[:, n % 2, n // 2 * 512:n // 2 * 512 + 512], ps_d[:, n], ACT.Copy).then_inc(out_ready[1], 1)

        @block.vector
        def _(dve):
            def lo_g(n, i=0):
                dve.wait_ge(s_g_hi, n + 1 + 2 * i)
                dve.tensor_tensor(g_lo[:, n % 2], g_raw[:, n % 2], f32(g_hi[:, n % 2]), ALU.subtract).then_inc(s_g_lo, 1)

            def lo_u(n, i=0):
                dve.wait_ge(s_u_hi, n + 1 + 2 * i)
                dve.tensor_tensor(u_lo[:, n % 2], u_raw[:, n % 2], f32(u_hi[:, n % 2]), ALU.subtract).then_inc(s_u_lo, 1)

            def lo_d(n, i=0):
                dve.wait_ge(s_d_hi, n + 1 + 2 * i)
                dve.tensor_tensor(d_lo[:, n % 2], d_raw[:, n % 2], f32(d_hi[:, n % 2]), ALU.subtract).then_inc(s_d_lo, 1)

            def mod_step(v, k, i=0):
                raw = {1: g_raw, 2: u_raw}.get(v, m_raw)
                arrived = {1: g_in, 2: u_in}.get(v, m_in)
                h = k // 4
                if k % 4 == 0:
                    dve.wait_ge(arrived[h], (16 * (v - 1) if v >= 3 else 16) + 32 * i)
                wk = raw[:, h].rearrange("p k n -> p (k n)")[:, (k % 4) * MOD_COLS:(k % 4 + 1) * MOD_COLS]
                if k == 0:
                    if v >= 1:
                        dve.wait_ge(turned_ready, v + 2 * i)
                    dve.tensor_scalar(acc[:], wk, csilu[:, 0:1], None, ALU.mult).then_inc(acc_step, 1)
                else:
                    dve.wait_ge(acc_step, 8 * v + k + 16 * i)
                    dve.scalar_tensor_tensor(out=acc[:], in0=wk, scalar=csilu[:, k:k + 1], in1=acc[:],
                                             op0=ALU.mult, op1=ALU.add).then_inc(acc_step, 1)

            def mod_turn(v, i=0):
                dve.wait_ge(acc_step, 8 * v + 8 + 16 * i)
                if v >= 1:
                    dve.wait_ge(part_ready, v + 2 * i)
                dve.transpose(turned[:], acc[:]).then_inc(turned_ready, 1)

            def mod_sum(v, i=0):
                dve.wait_ge(turned_ready, v + 1 + 2 * i)
                dve.tensor_reduce(part[:, bass.ds(unit_at(v) + 2 * i, 1)], turned[:].rearrange("p (m q) -> p m q", q=SQ),
                                  AX.X, ALU.add).then_inc(part_ready, 1)

            def mod_unit(v, first=0):
                for k in range(first, KT):
                    mod_step(v, k)
                mod_turn(v)
                mod_sum(v)

            def mod_out(group):
                first, end = MOD_GROUPS[group]
                dve.wait_ge(reduced, group + 1)
                dve.tensor_tensor(mcol[:, first * MOD_SUB:end * MOD_SUB], ps_mod[:, 0:(end - first) * MOD_SUB],
                                  cols[:, MOD_B + first * MOD_SUB:MOD_B + end * MOD_SUB], ALU.add).then_inc(mcol_ready, 1)

            def block_prod(f, b, i=0):
                e = NB * f + b
                dve.wait_ge(gated_ready, e + 1 + 2 * i)
                if e >= 1:
                    dve.wait_ge(a_lo_ready, e + 2 * i)
                dve.tensor_tensor(prod, gated, (ps_u if b else first_u)[:], ALU.mult).then_inc(prod_ready, 1)

            def block_lo(f, b, i=0):
                e = NB * f + b
                dve.wait_ge(a_hi_ready, e + 1 + 2 * i)
                dve.tensor_tensor(a_lo[:, b % 2].rearrange("p j t -> p (j t)"), prod,
                                  f32(a_hi[:, b % 2].rearrange("p j t -> p (j t)")), ALU.subtract).then_inc(a_lo_ready, 1)

            def steady(f, b, i=0):
                block_prod(f, b, i)
                last = MOD_AT[f] + b - 1 if MOD_AT[f] and 1 <= b <= MOD_LAST[f] + 1 else None
                this = MOD_AT[f] + b if b <= MOD_LAST[f] else None
                early = 2 if b == 0 and f in (1, 2) else 0
                if last is not None:
                    mod_turn(last, i)
                for k in range(early):
                    mod_step(this, k, i)
                block_lo(f, b, i)
                lo_g(G0[f] + b + 2, i)
                if last is not None:
                    mod_sum(last, i)
                if this is not None:
                    mod_step(this, early, i)
                lo_u(U0[f] + b + 2, i)
                if this is not None:
                    mod_step(this, early + 1, i)
                lo_d(D0[f] + b + 1, i)
                if this is not None:
                    for k in range(early + 2, KT):
                        mod_step(this, k, i)
                if (f, b) == (0, NB - 2):
                    mod_unit(MOD_MORE)

            def block_out(f, b):
                block_prod(f, b)
                block_lo(f, b)

            def middle(f):
                steady(f, 0)
                with dve.Fori(0, LOOPS) as i:
                    steady(f, 1, i)
                    steady(f, 2, i)

            def last_block(f):
                block_out(f, NB - 1)
                mod_turn(MOD_AT[f] + NB - 2)
                mod_sum(MOD_AT[f] + NB - 2)
                lo_g(G0[f] + NB + 1)

            def norm_coef(s, layer, k):
                g = NORM_G + (layer * 3 + k) * KT
                m = mod_at(layer, 3 * k + 1)
                dve.scalar_tensor_tensor(out=coef[:], in0=mcol[:, m:m + KT], scalar=1.0, in1=cols[:, g:g + KT],
                                         op0=ALU.add, op1=ALU.mult).then_inc(coef_ready, 1)

            def residual(s, wait, gate):
                for q in range(PAIRS):
                    dve.wait_ge(*wait(q))
                    for k in (2 * q, 2 * q + 1):
                        ins = dve.scalar_tensor_tensor(out=xs[:, k], in0=ps_d[:, q, (k % 2) * L:(k % 2 + 1) * L],
                                                       scalar=gate[:, k:k + 1], in1=xs[:, k], op0=ALU.mult, op1=ALU.add)
                    ins.then_inc(x_ready, 1)

            def norm_rstd(r):
                dve.wait_ge(root_ready, r + 1)
                dve.reciprocal(rstd, rstd).then_inc(rstd_ready, 1)
                dve.wait_ge(rstd_ready, r + 1)

            def scale_tile(r, k, source):
                if k >= 2:
                    if r in (NORM_OF_STAGE[6], LN_NORM):
                        dve.wait_ge(operand_ready, KT * r + k - 1)
                    else:
                        dve.wait_ge(h_hi_ready, KT * r + k - 1)
                dve.tensor_tensor(scaled[k % 2], source[:, k], rstd, ALU.mult).then_inc(scaled_ready, 1)

            def pool_copy(g):
                dve.wait_ge(rows_psum, g + 1)
                if g >= 2:
                    dve.wait_ge(bank_ready, 3 + g - 1)
                dve.tensor_copy(pool_rows[g % 2], (ps_g, ps_u)[g % 2][:]).then_inc(rows_ready, 1)

            def norm_tiles(r):
                for k in range(KT):
                    scale_tile(r, k, xs)
                    if k >= 1:
                        norm_lo(r, k - 1)
                    if r == 1 and k in (4, 6):
                        pool_copy(k // 2 - 2)
                norm_lo(r, KT - 1)

            def norm_lo(r, k):
                dve.wait_ge(h_hi_ready, KT * r + k + 1)
                dve.tensor_tensor(h_lo[:, k], wide[:, k, PAD:PAD + L], f32(h_hi[:, k]), ALU.subtract).then_inc(h_lo_ready, 1)

            def stage_norm(s):
                norm_rstd(NORM_OF_STAGE[s])
                norm_tiles(NORM_OF_STAGE[s])

            def half_gate(layer, k):
                m = mod_at(layer, 3 * k + 2)
                dve.tensor_scalar(gcoef[:], mcol[:, m:m + KT], 0.5, None, ALU.mult).then_inc(coef_ready, 1)

            def ffn_bank(f):
                k = [0, 2, 3, 5][f]
                return lambda q: (bank_ready, 3 * k + q + 1) if q < PAIRS - 1 else (d_done, D0[f] + NB)

            dve.wait_ge(edge_ready, 2 * len(POOL_WINDOWS))
            dve.reciprocal(edge[:], edge[:]).then_inc(share_ready, 1)
            dve.wait_ge(csilu_ready, 1)
            mod_unit(0)
            mod_unit(1)
            mod_unit(2)
            dve.wait_ge(cols_psum, 1)
            dve.tensor_copy(cols[:], ps_u[:, 0:N_COLS]).then_inc(cols_ready, 1)
            norm_rstd(0)
            mod_unit(3)
            lo_g(0)
            mod_out(0)
            dve.wait_ge(mcol_ready, 1)
            dve.wait_ge(cols_ready, 1)
            norm_coef(0, 0, 0)
            dve.wait_ge(coef_ready, 1)
            norm_tiles(0)
            lo_u(0)
            lo_g(1)
            lo_u(1)
            lo_d(0)

            middle(0)
            steady(0, NB - 2)
            block_out(0, NB - 1)
            mod_unit(MOD_MORE + 1)
            mod_out(1)
            dve.wait_ge(mcol_ready, 2)
            norm_coef(1, 0, 1)
            half_gate(0, 0)
            dve.wait_ge(coef_ready, 3)
            residual(1, ffn_bank(0), gcoef)
            for k in range(PRE_STEPS):
                mod_step(MOD_MORE + 2, k)
            stage_norm(1)
            pool_copy(2)
            pool_copy(3)
            m = mod_at(0, 5)
            dve.tensor_tensor(gcoef[:], mcol[:, m:m + KT], cols[:, POOL_SC:POOL_SC + KT], ALU.mult).then_inc(coef_ready, 1)
            dve.wait_ge(coef_ready, 4)
            residual(2, lambda q: (bank_ready, 3 + q + 1) if q < PAIRS - 1 else (gu_done, NB + 1), gcoef)
            mod_unit(MOD_MORE + 2, PRE_STEPS)
            lo_g(NB + 1)
            mod_out(2)
            dve.wait_ge(mcol_ready, 3)
            norm_coef(2, 0, 2)
            lo_u(NB + 1)
            dve.wait_ge(coef_ready, 5)
            stage_norm(2)
            lo_d(NB)
            lo_g(NB + 2)

            middle(1)
            steady(1, NB - 2)
            last_block(1)
            mod_out(3)
            dve.wait_ge(mcol_ready, 4)
            norm_coef(3, 1, 0)
            half_gate(0, 2)
            dve.wait_ge(coef_ready, 7)
            residual(3, ffn_bank(1), gcoef)
            lo_u(U0[1] + NB + 1)
            stage_norm(3)
            lo_d(D0[1] + NB)

            middle(2)
            steady(2, NB - 2)
            last_block(2)
            mod_out(4)
            dve.wait_ge(mcol_ready, 5)
            norm_coef(4, 1, 1)
            half_gate(1, 0)
            dve.wait_ge(coef_ready, 9)
            residual(4, ffn_bank(2), gcoef)
            lo_u(U0[2] + NB + 1)
            stage_norm(4)
            lo_d(D0[2] + NB)

            def glu(b):
                dve.wait_ge(glu_gate_ready, b + 1)
                src = ps_g if b % 2 == 0 else ps_d[:, 0]
                for k in (0, 1):
                    dve.tensor_tensor(wide[:, 2 * b + k, PAD:PAD + L], gated[:, k * L:(k + 1) * L],
                                      src[:, k * L:(k + 1) * L], ALU.mult).then_inc(glu_ready, 1)

            taps_done = [0]

            def taps(tiles, first, end):
                if first == 0:
                    dve.wait_ge(glu_ready, max(tiles) + 1)
                for w in range(first, end):
                    for k in tiles:
                        col = cols[:, DW + w * KT + k:DW + w * KT + k + 1]
                        src = wide[:, k, w:w + L]
                        if w == 0:
                            dve.tensor_scalar(conv[:, k], src, col, None, ALU.mult).then_inc(tap_step, 1)
                        else:
                            dve.wait_ge(tap_step, taps_done[0] - len(tiles) + 1)
                            dve.scalar_tensor_tensor(out=conv[:, k], in0=src, scalar=col, in1=conv[:, k],
                                                     op0=ALU.mult, op1=ALU.add).then_inc(tap_step, 1)
                        taps_done[0] += 1

            glu(0)
            taps((0, 1), 0, 3)
            lo_g(GC + 2)
            lo_u(UC + 2)
            taps((0, 1), 3, 7)
            glu(1)
            taps((0, 1), 7, 9)
            lo_g(GC + 3)
            lo_u(UC + 3)
            taps((0, 1), 9, 14)
            glu(2)
            taps((0, 1), 14, 26)
            glu(3)
            taps((0, 1), 26, TAPS)
            taps((2, 3, 4), 0, TAPS)
            dve.wait_ge(mu_ready, 1)
            for q in range(PAIRS):
                dve.tensor_tensor(conv[:, 2 * q:2 * q + 2], conv[:, 2 * q:2 * q + 2],
                                  ps_mod[:, 0:L].unsqueeze(1).to_broadcast([P, 2, L]), ALU.subtract).then_inc(centred, 1)
            lo_d(DC + 1)
            norm_rstd(LN_NORM)
            for k in range(KT):
                scale_tile(LN_NORM, k, conv)
                if k >= 1:
                    norm_lo(LN_NORM, k - 1)
            norm_lo(LN_NORM, KT - 1)
            lo_g(G0[3])
            lo_d(DC + 2)
            lo_u(U0[3])
            lo_d(DC + 3)
            lo_g(G0[3] + 1)
            norm_coef(5, 1, 2)
            dve.wait_ge(coef_ready, 10)
            m = mod_at(1, 5)
            residual(5, lambda q: (bank_ready, 3 * 4 + q + 1) if q < PAIRS - 1 else (d_done, DC + NC), mcol[:, m:m + KT])
            lo_u(U0[3] + 1)
            stage_norm(5)
            lo_d(D0[3])

            middle(3)
            block_out(3, NB - 2)
            lo_d(D0[3] + NB - 1)
            block_out(3, NB - 1)
            half_gate(1, 2)
            dve.wait_ge(coef_ready, 11)
            residual(6, ffn_bank(3), gcoef)
            r = NORM_OF_STAGE[6]
            norm_rstd(r)
            scale_tile(r, 0, xs)
            for k in range(1, KT):
                scale_tile(r, k, xs)
            for n in (0, 2):
                dve.wait_ge(out_psum, n + 1)
                dve.tensor_copy(out_rows[:, n % 2, n // 2 * 512:n // 2 * 512 + 512], ps_d[:, n]).then_inc(out_ready[0], 1)

        @block.tensor
        def _(pe):
            def mm3(dst, w_hi, w_lo, m_hi, m_lo, start, stop):
                pe.matmul(dst, w_hi, m_hi, start=start, stop=False, skip_group_check=True)
                pe.matmul(dst, w_hi, m_lo, start=False, stop=False, skip_group_check=True)
                return pe.matmul(dst, w_lo, m_hi, start=False, stop=stop, skip_group_check=True)

            def gate_up(g, u, lo_from, i=0, banks=None):
                dst_g, dst_u = banks or (ps_g, ps_u)
                pe.wait_ge(s_g_lo, g + 1 + 2 * i)
                halves = [(dst_g, g_hi, g_lo, g % 2), (dst_u, u_hi, u_lo, u % 2)]
                if g > 0:
                    pe.wait_ge(s_u_lo, u + 1 + 2 * i)
                    order = [(k, halves) for k in range(KT)]
                else:
                    order = [(k, [half]) for half in halves for k in range(KT)]
                for n, (k, todo) in enumerate(order):
                    if lo_from is not None and n < KT:
                        pe.wait_ge(h_lo_ready, lo_from + k + 1)
                    if n == KT:
                        pe.wait_ge(s_u_lo, 1)
                    for dst, hi, lo, slot in todo:
                        for j in range(SUB):
                            mm = mm3(dst[:, j * L:(j + 1) * L], hi[:, slot, k, j * P:(j + 1) * P],
                                     lo[:, slot, k, j * P:(j + 1) * P], h_hi[:, k], h_lo[:, k],
                                     start=(k == 0 and j == 0), stop=(k == KT - 1))
                mm.then_inc(gu_done, 1)

            def ffn_block(f, b, i=0):
                e = NB * f + b
                if b == 0:
                    gate_up(G0[f], U0[f], KT * NORM_OF_STAGE[FFN_STAGE[f]], banks=(first_g, first_u))
                    return
                if b >= 2:
                    pe.wait_ge(prod_ready, e + 2 * i)
                gate_up(G0[f] + b, U0[f] + b, None, i)

            def mod_reduce(group):
                first, end = MOD_GROUPS[group]
                pe.wait_ge(part_ready, end)
                if group >= 1:
                    pe.wait_ge(mcol_ready, group)
                for m in range(P // SQ):
                    sums = part[:, first:end].rearrange("p v (j m) -> p m (v j)", m=P // SQ)[:, m]
                    mm = pe.matmul(ps_mod[:, 0:(end - first) * MOD_SUB], gather[:, P - SQ - SQ * m:2 * P - SQ - SQ * m],
                                   sums, start=(m == 0), stop=(m == P // SQ - 1), skip_group_check=True)
                mm.then_inc(reduced, 1)

            def down_unit(d, first, m_hi, m_lo, tiles, i=0, stop=False):
                for j in range(SUB):
                    for k in tiles:
                        mm = mm3(ps_d[:, k // 2, (k % 2) * L:(k % 2 + 1) * L], d_hi[:, d % 2, j, k * P:(k + 1) * P],
                                 d_lo[:, d % 2, j, k * P:(k + 1) * P], m_hi(j), m_lo(j),
                                 start=(first and j == 0 and k % 2 == 0), stop=(stop and j == SUB - 1))
                return mm

            def last_down(d, m_hi, m_lo, group=None):
                for q in range(PAIRS):
                    mm = down_unit(d, False, m_hi, m_lo, (2 * q, 2 * q + 1), stop=True)
                    mm.then_inc(bank_ready if q < PAIRS - 1 else d_done, 1)
                    if q == 0 and group is not None:
                        mod_reduce(group)

            def ffn_down(f, b, i=0):
                d = D0[f] + b
                pe.wait_ge(s_d_lo, d + 1 + 2 * i)
                pe.wait_ge(a_lo_ready, NB * f + b + 1 + 2 * i)
                m_hi, m_lo = (lambda j: a_hi[:, b % 2, j]), (lambda j: a_lo[:, b % 2, j])
                if b == NB - 1:
                    last_down(d, m_hi, m_lo, {1: 3, 2: 4}.get(f))
                else:
                    down_unit(d, b == 0, m_hi, m_lo, range(KT), i).then_inc(d_done, 1)

            def steady(f, b, i=0):
                ffn_block(f, b, i)
                ffn_down(f, b - 1, i)

            def ffn(f):
                ffn_block(f, 0)
                steady(f, 1)
                with pe.Fori(0, LOOPS) as i:
                    steady(f, 2, i)
                    steady(f, 3, i)
                steady(f, NB - 1)
                if f == 0:
                    mod_reduce(1)
                ffn_down(f, NB - 1)

            def stat(r):
                for q in range(PAIRS):
                    pe.wait_ge(sq_ready, PAIRS * r + q + 1)
                    for k in (0, 1):
                        mm = pe.matmul(ps_stat[:, 0:L], mean_w[:], sq[q % 2][:, k * L:(k + 1) * L],
                                       start=(q == 0 and k == 0), stop=(q == PAIRS - 1 and k == 1), skip_group_check=True)
                    mm.then_inc(stat_step, 1)

            def keep_clock():
                for n in range(WARM):
                    pe.matmul(ps_g[:, 0:P], mean_w[:], mean_w[:], start=True, stop=True, skip_group_check=True)

            pe.wait_ge(consts_ready, 1)
            pe.wait_ge(c_in, 16)
            pe.transpose(ps_mod[:, 0:KT], c_rows, ident[0:KT, 0:KT]).then_inc(c_psum, 1)
            pe.wait_ge(d_in[1], 16)
            for q in range(PAIRS):
                for k in (0, 1):
                    for a in range(L // P):
                        mm = pe.transpose(ps_d[:, q, k * L + a * P:k * L + (a + 1) * P],
                                          x_rows[:, a, (2 * q + k) * P:(2 * q + k + 1) * P], ident[:])
                mm.then_inc(xt_ready, 1)
            pe.wait_ge(vec_in, 16 * VEC_LOADS)
            at = 0
            for r, n in enumerate((MOD_B, N_MOD * KT, N_MOD * KT, TAPS * KT // 2, TAPS * KT // 2)):
                mm = pe.transpose(ps_u[:, at:at + n], vec_rows[0:n, r, :], ident[0:n, 0:n])
                at += n
            mm.then_inc(cols_psum, 1)
            pe.wait_ge(consts_ready, CONSTS)
            stat(0)
            mod_reduce(0)

            ffn(0)
            stat(1)
            keep_clock()
            pe.wait_ge(s_g_lo, NB + 1)
            slot = NB % 2
            pe.wait_ge(prod_ready, NB)
            pe.wait_ge(consts_ready, POOL_CONSTS)

            def pool_product(g):
                pe.wait_ge(h_lo_ready, KT * 1 + 2 * g + 2)
                if g >= 2:
                    pe.wait_ge(rows_ready, g - 1)
                for a in range(L // P):
                    for j in range(SUB):
                        at = slice(P * a, P * (a + 1))
                        mm = mm3((ps_g, ps_u)[g % 2][:, a * BLK:(a + 1) * BLK], h_hi[:, 2 * g + j, at], h_lo[:, 2 * g + j, at],
                                 g_hi[:, slot, 2 * g + j], g_lo[:, slot, 2 * g + j], start=(a == 0 and j == 0), stop=(j == SUB - 1))
                mm.then_inc(rows_psum, 1)

            def pool_tokens(g):
                pe.wait_ge(rows_ready, g + 1)
                for m in range(SUB):
                    for a in range(L // P):
                        reach = slice(m * L + (L - REACH) * a, m * L + (L - REACH) * a + REACH)
                        mm = pe.matmul(ps_d[:, g, reach], pool_rows[g % 2][:, a * BLK + m * P:a * BLK + (m + 1) * P],
                                       pool_mat[:, g, a], start=(m == 0 and a == 0), stop=(a == L // P - 1), skip_group_check=True)
                mm.then_inc(bank_ready if g < PAIRS - 1 else gu_done, 1)

            pool_product(0)
            pool_product(1)
            pool_tokens(0)
            pool_product(2)
            pool_tokens(1)
            pool_product(3)
            pool_tokens(2)
            pool_tokens(3)
            stat(2)
            mod_reduce(2)
            keep_clock()

            for f in (1, 2):
                ffn(f)
                stat(NORM_OF_STAGE[f + 2])
                keep_clock()

            for b in range(NC):
                if b >= 2:
                    pe.wait_ge(glu_ready, 2 * (b - 1))
                gate_up(GC + b, UC + b, KT * 4 if b == 0 else None, banks=None if b % 2 == 0 else (ps_d[:, 0], ps_d[:, 1]))
            n = 0
            for t in CONV_TILES_ON_PE:
                pe.wait_ge(glu_ready, t + 1)
                for w in range(TAPS):
                    pe.wait_ge(diag_ready, n + 1)
                    mm = pe.matmul(ps_d[:, CONV_BANK[t], 0:L], diag[:, n % DIAG_SLOTS], wide[:, t, w:w + L],
                                   start=(w == 0), stop=(w == TAPS - 1), skip_group_check=True)
                    mm.then_inc(diag_used, 1)
                    n += 1
            for n, k in enumerate((0, 1) + CONV_TILES_ON_PE + (2, 3, 4)):
                if k in CONV_TILES_ON_PE:
                    pe.wait_ge(conv_ready, CONV_TILES_ON_PE.index(k) + 1)
                else:
                    pe.wait_ge(tap_step, TAPS * 2 - 1 + k if k < 2 else TAPS * 5 - 4 + k)
                mm = pe.matmul(ps_mod[:, 0:L], mean_w[:], conv[:, k], start=(n == 0), stop=(n == KT - 1), skip_group_check=True)
            mm.then_inc(mu_ready, 1)
            stat(LN_NORM)
            keep_clock()
            for b in range(NC):
                pe.wait_ge(s_d_lo, DC + b + 1)
                pe.wait_ge(h_lo_ready, KT * LN_NORM + 2 * b + 2)
                m_hi, m_lo = (lambda j: h_hi[:, 2 * b + j]), (lambda j: h_lo[:, 2 * b + j])
                if b == NC - 1:
                    last_down(DC + b, m_hi, m_lo)
                else:
                    down_unit(DC + b, b == 0, m_hi, m_lo, range(KT)).then_inc(d_done, 1)
            stat(NORM_OF_STAGE[5])
            keep_clock()

            ffn(3)
            r = NORM_OF_STAGE[6]
            stat(r)
            for n in range(PAIRS):
                a, half = n % 2, n // 2
                for k in range(KT // 2):
                    dt = half * (KT // 2) + k
                    pe.wait_ge(operand_ready, KT * r + dt + 1)
                    mm = pe.transpose(ps_d[:, n, k * P:(k + 1) * P], wide[:, dt, PAD + a * P:PAD + (a + 1) * P], ident[:])
                mm.then_inc(out_psum, 1)


_INS = ['x', 'c', 'mod_w', 'mod_b', 'norm_g', 'final_g', 'ffn_w_gate', 'ffn_w_up', 'ffn_w_down', 'pool_w',
        'pool_scale', 'conv_w_in', 'conv_dw', 'conv_ln_g', 'conv_ln_b', 'conv_w_out']


def kernel(**inputs):
    import numpy as _np
    import concourse.bacc as _bacc
    from concourse import mybir as _mybir
    from concourse.bass_utils import run_bass_kernel_spmd as _run

    nc = _bacc.Bacc("TRN2", target_bir_lowering=False, num_devices=1,
                    dynamic_dma_scratch_size=512)
    arrays, args = {}, []
    for name in _INS:
        a = _np.ascontiguousarray(inputs[name])
        arrays[f"in_{name}_dram"] = a
        args.append(nc.dram_tensor(f"in_{name}_dram", a.shape, _mybir.dt.from_np(a.dtype), kind="ExternalInput").ap())
    x = inputs['x']
    out = nc.dram_tensor("out_0_dram", x.shape, _mybir.dt.from_np(_np.dtype(x.dtype)), kind="ExternalOutput").ap()
    backbone_kernel(nc, *args, out)
    r = _run(nc, [arrays], core_ids=[0])
    return r.results[0]["out_0_dram"]
```
